# Optimizing a Trainium2 kernel written in Bass

```python
import math, functools
import jax, jax.numpy as jnp
from jax import lax
import numpy as np

D_MODEL = 2048
BATCH = 1
SEQ = 512
DEPTH = 1
DEC_BATCH = 8
DEC_SEQ = 4
PAST_LEN = 4096
PAGE_SIZE = 128

N_META = 16
NORM_EPS = 1e-6
A_WIDTH = D_MODEL
A_HEAD = 64
A_HEADS = A_WIDTH // A_HEAD
DECAY_LORA = max(32, int(round(1.8 * D_MODEL ** 0.5 / 32)) * 32)
AAA_LORA = max(32, int(round(1.8 * D_MODEL ** 0.5 / 32)) * 32)
LNX_EPS = 64e-5
B_HEADS = 4
B_KDIM = D_MODEL // 2
B_VDIM = D_MODEL
B_HK = B_KDIM // B_HEADS
B_HV = B_VDIM // B_HEADS
GATE_LORA = 16
GATE_TAU = 16.0
CHUNK = 64
SHIFT_COLS = 3 * A_WIDTH + DECAY_LORA + AAA_LORA
SHIFT_SPLITS = (A_WIDTH, 2 * A_WIDTH, 3 * A_WIDTH, 3 * A_WIDTH + DECAY_LORA)
REST_SIZES = (A_WIDTH, B_KDIM, B_KDIM, B_VDIM, GATE_LORA, B_VDIM, D_MODEL, D_MODEL)
REST_SPLITS = tuple(int(i) for i in np.cumsum(REST_SIZES)[:-1])
N_COLS = SHIFT_COLS + sum(REST_SIZES)

kernel_name = "hybrid_rwkv7_gla_gated_decoder_step"

def _rms_norm(x, g):
    xf = x.astype(jnp.float32)
    y = xf * lax.rsqrt(jnp.mean(xf * xf, axis=-1, keepdims=True) + NORM_EPS)
    return (y * g.astype(jnp.float32)).astype(x.dtype)

def _rwkv7_branch(zs, za, state, buf, mu, w0, w2, a0, a2, k_k, k_a, r_k, lnx_w, lnx_b):
    n, t, _ = zs.shape
    f32 = jnp.float32
    zf = zs.astype(f32)
    prev = jnp.concatenate([buf[:, None, :].astype(f32), zf[:, :-1]], axis=1)
    xs = zf + (prev - zf) * mu.astype(f32)
    r, k, v, w_lo, a_lo = jnp.split(xs, SHIFT_SPLITS, axis=-1)
    w = -jax.nn.softplus(-(w0 + jnp.tanh(w_lo) @ w2)) - 0.5
    decay = jnp.exp(-jnp.exp(w))
    a = jax.nn.sigmoid(a0 + a_lo @ a2)
    hd = lambda u: u.reshape(n, t, A_HEADS, A_HEAD)
    kk = hd(k * k_k)
    kk = kk / jnp.maximum(jnp.sqrt(jnp.sum(kk * kk, axis=-1, keepdims=True)), 1e-12)
    k = k * (1.0 + (a - 1.0) * k_a)
    r, k, v, decay, a = hd(r), hd(k), hd(v), hd(decay), hd(a)
    a_vec = -kk
    b_vec = kk * a

    def step(S, inp):
        r_t, w_t, k_t, v_t, a_t, b_t = inp
        sa = jnp.einsum('nhvk,nhk->nhv', S, a_t)
        S = S * w_t[:, :, None, :] + sa[..., None] * b_t[:, :, None, :] + v_t[..., None] * k_t[:, :, None, :]
        return S, jnp.einsum('nhvk,nhk->nhv', S, r_t)

    seq = tuple(jnp.swapaxes(u, 0, 1) for u in (r, decay, k, v, a_vec, b_vec))
    s_fin, y = lax.scan(step, state.astype(f32), seq)
    y = jnp.swapaxes(y, 0, 1)
    mean = jnp.mean(y, axis=-1, keepdims=True)
    var = jnp.mean(jnp.square(y - mean), axis=-1, keepdims=True)
    y = ((y - mean) * lax.rsqrt(var + LNX_EPS)).reshape(n, t, A_WIDTH) * lnx_w + lnx_b
    bonus = jnp.sum(r * k * r_k.astype(f32), axis=-1, keepdims=True) * v
    y = (y + bonus.reshape(n, t, A_WIDTH)) * jax.nn.silu(za.astype(f32))
    return y.astype(zs.dtype), s_fin, zs[:, -1]

def _gla_branch(q, k, v, g_lo, zb, state, gk_w2, gk_b, norm_w, front):
    n, t, _ = q.shape
    f32 = jnp.float32
    g = jax.nn.log_sigmoid(g_lo.astype(f32) @ gk_w2 + gk_b) / GATE_TAU
    q = q.astype(f32) * (B_HK ** -0.5)
    total = front + t
    c = min(CHUNK, total)
    n_chunks = -(-total // c)
    back = n_chunks * c - total

    def prep(u, d):
        u = jnp.pad(u.astype(f32), ((0, 0), (front, back), (0, 0)))
        return u.reshape(n, n_chunks, c, B_HEADS, d).transpose(1, 0, 3, 2, 4)

    mask = jnp.tril(jnp.ones((c, c), dtype=bool))[:, :, None]

    def step(S, inp):
        qc, kc, vc, gc = inp
        b = jnp.cumsum(gc, axis=2)
        o = jnp.einsum('nhtk,nhkv->nhtv', qc * jnp.exp(b), S)
        diff = b[:, :, :, None, :] - b[:, :, None, :, :]
        dec = jnp.exp(jnp.where(mask, diff, -jnp.inf))
        att = jnp.einsum('nhtk,nhsk,nhtsk->nhts', qc, kc, dec)
        o = o + jnp.einsum('nhts,nhsv->nhtv', att, vc)
        b_last = b[:, :, -1:, :]
        S = S * jnp.exp(b_last)[:, :, 0, :, None] + jnp.einsum('nhsk,nhsv->nhkv', kc * jnp.exp(b_last - b), vc)
        return S, o

    s_fin, o = lax.scan(step, state.astype(f32), (prep(q, B_HK), prep(k, B_HK), prep(v, B_HV), prep(g, B_HK)))
    o = o.transpose(1, 0, 3, 2, 4).reshape(n, n_chunks * c, B_HEADS, B_HV)[:, front:front + t]
    o = o * lax.rsqrt(jnp.mean(o * o, axis=-1, keepdims=True) + NORM_EPS) * norm_w.astype(f32)
    o = o.reshape(n, t, B_VDIM) * jax.nn.silu(zb.astype(f32))
    return o.astype(zb.dtype), s_fin

def _trunk(x, st_rwkv, st_shift, st_gla, gla_front, params):
    (norm_pre, w_in, rwkv_mu, rwkv_w0, rwkv_w2, rwkv_a0, rwkv_a2, rwkv_k_k, rwkv_k_a, rwkv_r_k,
     rwkv_lnx_w, rwkv_lnx_b, gla_gk_w2, gla_gk_b, gla_norm_w, w_out, norm_post) = params
    new_r, new_s, new_g = [], [], []
    for l in range(DEPTH):
        h = _rms_norm(x, norm_pre[l])
        z = h @ w_in[l]
        zs = z[..., :SHIFT_COLS]
        za, qb, kb, vb, glo, zb, ga, gb = jnp.split(z[..., SHIFT_COLS:], REST_SPLITS, axis=-1)
        oa, sr, ss = _rwkv7_branch(zs, za, st_rwkv[l], st_shift[l], rwkv_mu[l], rwkv_w0[l], rwkv_w2[l],
                                   rwkv_a0[l], rwkv_a2[l], rwkv_k_k[l], rwkv_k_a[l], rwkv_r_k[l],
                                   rwkv_lnx_w[l], rwkv_lnx_b[l])
        ob, sg = _gla_branch(qb, kb, vb, glo, zb, st_gla[l], gla_gk_w2[l], gla_gk_b[l], gla_norm_w[l], gla_front)
        m = jax.nn.sigmoid(ga) * oa + jax.nn.sigmoid(gb) * ob
        x = x + _rms_norm(m @ w_out[l], norm_post[l])
        new_r.append(sr.astype(x.dtype))
        new_s.append(ss.astype(x.dtype))
        new_g.append(sg.astype(x.dtype))
    return x, jnp.stack(new_r), jnp.stack(new_s), jnp.stack(new_g)

def setup_inputs(seed: int = 0) -> dict:
    key = jax.random.key(seed)
    ks = jax.random.split(key, 24)
    nrm = lambda k, s, sc: jax.random.normal(k, s, jnp.float32) * sc
    D = D_MODEL
    return {
        "x_prompt": nrm(ks[0], (BATCH, SEQ, D), 1.0),
        "x_sample": nrm(ks[1], (DEC_BATCH, DEC_SEQ, D), 1.0),
        "state_rwkv": nrm(ks[2], (DEPTH, DEC_BATCH, A_HEADS, A_HEAD, A_HEAD), 0.5),
        "state_shift": nrm(ks[3], (DEPTH, DEC_BATCH, SHIFT_COLS), 1.0),
        "state_gla": nrm(ks[4], (DEPTH, DEC_BATCH, B_HEADS, B_HK, B_HV), 1.0),
        "meta_tokens": nrm(ks[5], (N_META, D), 1.0),
        "norm_pre": 1.0 + nrm(ks[6], (DEPTH, D), 0.05),
        "w_in": nrm(ks[7], (DEPTH, D, N_COLS), D ** -0.5),
        "rwkv_mu": jax.random.uniform(ks[8], (DEPTH, SHIFT_COLS), jnp.float32, 0.0, 1.0),
        "rwkv_w0": jax.random.uniform(ks[9], (DEPTH, A_WIDTH), jnp.float32, -6.0, 0.0),
        "rwkv_w2": nrm(ks[10], (DEPTH, DECAY_LORA, A_WIDTH), DECAY_LORA ** -0.5),
        "rwkv_a0": nrm(ks[11], (DEPTH, A_WIDTH), 0.1),
        "rwkv_a2": nrm(ks[12], (DEPTH, AAA_LORA, A_WIDTH), AAA_LORA ** -0.5),
        "rwkv_k_k": 0.85 + nrm(ks[13], (DEPTH, A_WIDTH), 0.05),
        "rwkv_k_a": 1.0 + nrm(ks[14], (DEPTH, A_WIDTH), 0.05),
        "rwkv_r_k": nrm(ks[15], (DEPTH, A_HEADS, A_HEAD), 0.1),
        "rwkv_lnx_w": 1.0 + nrm(ks[16], (DEPTH, A_WIDTH), 0.05),
        "rwkv_lnx_b": nrm(ks[17], (DEPTH, A_WIDTH), 0.01),
        "gla_gk_w2": nrm(ks[18], (DEPTH, GATE_LORA, B_KDIM), GATE_LORA ** -0.5),
        "gla_gk_b": nrm(ks[19], (DEPTH, B_KDIM), 0.1),
        "gla_norm_w": 1.0 + nrm(ks[20], (DEPTH, B_HV), 0.05),
        "w_out": nrm(ks[21], (DEPTH, D, D), D ** -0.5),
        "norm_post": 1.0 + nrm(ks[22], (DEPTH, D), 0.05),
    }

def reference(x_prompt, x_sample, state_rwkv, state_shift, state_gla, meta_tokens, norm_pre, w_in, rwkv_mu,
              rwkv_w0, rwkv_w2, rwkv_a0, rwkv_a2, rwkv_k_k, rwkv_k_a, rwkv_r_k, rwkv_lnx_w, rwkv_lnx_b,
              gla_gk_w2, gla_gk_b, gla_norm_w, w_out, norm_post):
    params = (norm_pre, w_in, rwkv_mu, rwkv_w0, rwkv_w2, rwkv_a0, rwkv_a2, rwkv_k_k, rwkv_k_a, rwkv_r_k,
              rwkv_lnx_w, rwkv_lnx_b, gla_gk_w2, gla_gk_b, gla_norm_w, w_out, norm_post)
    dt = x_prompt.dtype
    meta = jnp.broadcast_to(meta_tokens.astype(dt)[None], (x_prompt.shape[0], N_META, D_MODEL))
    xp = jnp.concatenate([meta, x_prompt], axis=1)
    bp = x_prompt.shape[0]
    z_rwkv = jnp.zeros((DEPTH, bp, A_HEADS, A_HEAD, A_HEAD), dt)
    z_shift = jnp.zeros((DEPTH, bp, SHIFT_COLS), dt)
    z_gla = jnp.zeros((DEPTH, bp, B_HEADS, B_HK, B_HV), dt)
    hp, p_rwkv, p_shift, p_gla = _trunk(xp, z_rwkv, z_shift, z_gla, CHUNK - N_META, params)
    y_prompt = hp[:, N_META:]
    y_sample, s_rwkv, s_shift, s_gla = _trunk(x_sample, state_rwkv, state_shift, state_gla, 0, params)
    return (y_prompt, y_sample, p_rwkv, p_shift, p_gla, s_rwkv, s_shift, s_gla)


_drawn_inputs = setup_inputs


def setup_inputs(seed=0):
    import zlib

    import numpy as np

    out = dict(_drawn_inputs(seed))
    spreads = {}
    factors = {'rwkv_lnx_b': 8.0}
    for name, (base, spread) in spreads.items():
        noise = np.random.default_rng([zlib.crc32(name.encode()), seed]).standard_normal(out[name].shape)
        drawn = base * np.exp(spread * noise) if base else spread * noise
        out[name] = __import__('jax').numpy.asarray(drawn.astype(out[name].dtype))
    for name, factor in factors.items():
        out[name] = (out[name] * factor).astype(out[name].dtype)
    return out
```

```python
from contextlib import ExitStack
from itertools import chain

import numpy as np
import concourse.bass as bass
from concourse import mybir

F32 = mybir.dt.float32
F32R = mybir.dt.float32r
I32 = mybir.dt.int32
ACT = mybir.ActivationFunctionType
ALU = mybir.AluOpType
MUL, ADD, SUB, MIN, MAX = ALU.mult, ALU.add, ALU.subtract, ALU.min, ALU.max
ds = bass.ds

P = 128
D = 2048
KT = D // P
META, SEQ, NSEQ, TS = 16, 512, 8, 4
TP = META + SEQ
T = TP + NSEQ * TS
TOK = T - META
HALF = T // 2
C = 64
NC = 9
NF = 8
TAIL = TP - NF * C
LAST = T - NF * C
HEAD, LORA, GLORA = 64, 96, 16
SHIFT = 3 * D + 2 * LORA
NPAIR = D // P
BH, BK_, BV = 4, 256, 512
COL_ZA = SHIFT
COL_Q = COL_ZA + D
COL_K = COL_Q + D // 2
COL_V = COL_K + D // 2
COL_GLO = COL_V + D
COL_ZB = COL_GLO + GLORA
COL_GA = COL_ZB + D
COL_GB = COL_GA + D
ZW = 1 + TP + NSEQ * (TS + 1)
DV, DS, DG = 48, 23, 7
DED = 2
DCV, DCS, DCG = 61, 26, 1
DECAY = -0.5 * float(np.exp(-0.5))


class Signal:

    def __init__(self, ctx, nc, name, per=0):
        self.sem, self.name, self.per = ctx.enter_context(nc.semaphore(name)), name, per
        self.count = self.bias = 0

    def next(self, i):
        self.count += 1
        return self.at(i, self.count)

    def at(self, i, k):
        assert k + self.bias > 0, self.name
        return i * self.per + (k + self.bias)

    def close(self):
        assert self.count == self.per, (self.name, self.count)


def seqs(ap):
    return ap[:, TP:T].rearrange("p (s t) -> p s t", s=NSEQ)


def build(nc, x_prompt, x_sample, state_rwkv, state_shift, state_gla, meta_tokens, norm_pre, w_in, rwkv_mu, rwkv_w0,
          rwkv_w2, rwkv_a0, rwkv_a2, rwkv_k_k, rwkv_k_a, rwkv_r_k, rwkv_lnx_w, rwkv_lnx_b, gla_gk_w2, gla_gk_b,
          gla_norm_w, w_out, norm_post, y_prompt, y_sample, p_rwkv, p_shift, p_gla, s_rwkv, s_shift, s_gla):
    ctx = ExitStack()
    with ctx:
        def sb(name, shape, dt=F32):
            return ctx.enter_context(nc.sbuf_tensor(name, shape, dt))

        def sig(name, per=0):
            return Signal(ctx, nc, name, per)

        psum = ctx.enter_context(nc.psum_tensor("psum", [P, 8, 512], F32))
        bank = [psum[:, n, :] for n in range(8)]
        act_hi = sb("act_hi", [P, KT, T], F32R)
        act_lo = sb("act_lo", [P, KT, T], F32R)
        raw = [sb(f"raw{n}", [P, KT // 2, P]) for n in range(2)]
        w_hi = [sb(f"w_hi{n}", [P, KT, P], F32R) for n in range(2)]
        w_lo = [sb(f"w_lo{n}", [P, KT, P], F32R) for n in range(2)]
        ident = sb("ident", [P, P])
        head_ones = sb("head_ones", [P, P])
        params = sb("params", [P, 192])
        derived = sb("derived", [P, 48])
        shift_in = sb("shift_in", [P, NSEQ * 48 + 16])
        shift_out = sb("shift_out", [P, 50, 9])
        lora = [sb(f"lora{n}", [LORA, T]) for n in range(2)]
        chunk_start = sb("chunk_start", [P, T])
        tiny = sb("tiny", [P, 4])
        ARENA = (212863 - 71680 - 8192 - 32768 - 1024 - 768 - 192 - 1600 - 1800 - 4480 - 2240 - 16 - 512) // 4
        arena = sb("arena", [P, ARENA])
        ob_dram = nc.dram_tensor("ob_dram", [NPAIR, P, T], F32, kind="Internal").ap()
        m_dram = nc.dram_tensor("m_dram", [NPAIR, P, T], F32, kind="Internal").ap()

        class Arena:

            def __init__(self):
                self.at = 0

            def __call__(self, *shape):
                n = int(np.prod(shape))
                assert self.at + n <= ARENA, (self.at + n, ARENA)
                ap = arena[:, self.at:self.at + n]
                self.at += n
                if len(shape) == 2:
                    ap = ap.rearrange("p (a b) -> p a b", a=shape[0])
                if len(shape) == 3:
                    ap = ap.rearrange("p (a b c) -> p a b c", a=shape[0], b=shape[1])
                return ap

        MU_R, MU_K, MU_V, W0, A0, K_K, K_A, R_K, LN_W, LN_B = range(0, 160, 16)
        GK_B, NORM_W, MU_LO = 160, 168, 172

        def bc(ap, n, axis=1):
            u = ap.unsqueeze(axis)
            shape = list(u.shape)
            shape[axis] = n
            return u.to_broadcast(shape)

        ar = Arena()
        x_in = [ar(D) for _ in range(2)]
        norm_row = ar(D)
        stats = ar(16)
        prow = ar(6, P)
        load_x, load_c, load_n = [sig(f"load_x{n}") for n in range(5)], sig("load_constants"), sig("load_norm")
        a_ss, a_sqrt, a_rs, a_xs = sig("a_square_sum"), sig("a_root"), sig("a_rstd"), sig("a_normalised")
        a_tr, a_hi, a_lo, a_par, a_parc = sig("a_transposed"), sig("a_hi"), sig("a_lo"), sig("a_params_T"), sig("a_params")
        a_pool, a_ones, a_eps = sig("a_pool"), sig("a_ident"), sig("a_eps")
        v_order, s_order = sig("a_vector"), sig("a_scalar")
        waited = sig("waited")
        rows_of = [P, P, P, P, LAST]
        with nc.Block() as block:
            @block.sync
            def _(sp):
                sp.dma_start(norm_row[:, :], norm_pre[0:1, :].to_broadcast([P, D])).then_inc(load_n.sem, 16)
                for t in range(5):
                    x = x_in[t % 2]
                    if t >= 2:
                        sp.wait_ge(a_xs.sem, t - 1)
                        sp.wait_ge(a_tr.sem, 4 * (t - 1))
                    if t == 0:
                        sp.dma_start(x[0:META, :], meta_tokens[:, :]).then_inc(load_x[t].sem, 16)
                        sp.dma_start(x[META:P, :], x_prompt[0, 0:P - META, :]).then_inc(load_x[t].sem, 16)
                    elif t < 4:
                        sp.dma_start(x[:, :], x_prompt[0, t * P - META:(t + 1) * P - META, :]).then_inc(load_x[t].sem, 16)
                    else:
                        sp.dma_start(x[0:TAIL, :], x_prompt[0, SEQ - TAIL:SEQ, :]).then_inc(load_x[t].sem, 16)
                        sp.dma_start(x[TAIL:LAST, :], x_sample.rearrange("s t d -> (s t) d")).then_inc(load_x[t].sem, 16)

            @block.gpsimd
            def _(pool):
                mine, i = a_pool, 0
                pool.memset(prow, 0.0).then_inc(mine.sem, 1)
                pool.wait_ge(mine.sem, mine.next(i))
                two = lambda v: v[0].rearrange("(j c) -> j c", c=P)
                vectors = [(0, rwkv_mu[0, 0:3 * D].rearrange("(j c) -> j c", c=P)), (48, two(rwkv_w0)), (64, two(rwkv_a0)),
                           (80, two(rwkv_k_k)), (96, two(rwkv_k_a)), (112, rwkv_r_k[0].rearrange("(j h) c -> j (h c)", h=2))]
                n = 0
                for at, v in vectors:
                    pool.dma_start(prow[at:at + v.shape[0], 0, :], v).then_inc(load_c.sem, 16)
                    n += 1
                for at, v in [(0, two(rwkv_lnx_w)), (16, two(rwkv_lnx_b)), (32, two(gla_gk_b)), (40, two(gla_norm_w))]:
                    pool.dma_start(prow[at:at + v.shape[0], 1, :], v).then_inc(load_c.sem, 16)
                    n += 1
                pool.dma_start(prow[44:46, 1, 0:LORA], rwkv_mu[0, 3 * D:SHIFT].rearrange("(j c) -> j c", c=LORA)).then_inc(load_c.sem, 16)
                for s in range(NSEQ):
                    pool.dma_start(prow[48 + 2 * s:50 + 2 * s, 1, 0:LORA],
                                   state_shift[0, s, 3 * D:SHIFT].rearrange("(j c) -> j c", c=LORA)).then_inc(load_c.sem, 16)
                    at = s * 48
                    while at < (s + 1) * 48:
                        m = min((s + 1) * 48, (at // P + 1) * P) - at
                        src = state_shift[0, s, (at - s * 48) * P:(at - s * 48 + m) * P].rearrange("(j c) -> j c", c=P)
                        pool.dma_start(prow[at % P:at % P + m, 2 + at // P, :], src).then_inc(load_c.sem, 16)
                        n += 1
                        at += m
                n += 1 + NSEQ
                load_c.total = 16 * n
                pool.memset(head_ones[:, :], 0.0).then_inc(mine.sem, 1)
                pool.wait_ge(mine.sem, mine.next(i))
                pool.memset(head_ones[0:64, 0:64], 1.0).then_inc(mine.sem, 1)
                pool.wait_ge(mine.sem, mine.next(i))
                pool.memset(head_ones[64:P, 64:P], 1.0).then_inc(mine.sem, 1)
                pool.wait_ge(mine.sem, mine.next(i))
                pool.memset(chunk_start[:, :], 1.0).then_inc(mine.sem, 1)
                pool.wait_ge(mine.sem, mine.next(i))
                pool.memset(chunk_start[:, 0:NF * C].rearrange("p (c t) -> p c t", c=NF)[:, :, 0:1], 0.0).then_inc(mine.sem, 1)
                pool.wait_ge(mine.sem, mine.next(i))
                pool.memset(chunk_start[:, NF * C:NF * C + 1], 0.0).then_inc(mine.sem, 1)
                pool.wait_ge(mine.sem, mine.next(i))
                pool.memset(seqs(chunk_start)[:, :, 0:1], 0.0).then_inc(mine.sem, 1)
                pool.wait_ge(mine.sem, mine.next(i))
                pool.memset(ident[:, :], 0.0).then_inc(mine.sem, 1)
                pool.wait_ge(mine.sem, mine.next(i))
                pool.affine_select(out=ident[:, :], in_=ident[:, :], compare_op=ALU.not_equal, fill=1.0, base=0,
                                   pattern=[[-1, P]], channel_multiplier=1).then_inc(a_ones.sem, 1)
                pool.wait_ge(a_ones.sem, a_ones.next(i))

            @block.scalar
            def _(act):
                mine, i = s_order, 0
                act.wait_ge(a_eps.sem, 1)
                for t in range(5):
                    n = rows_of[t]
                    act.wait_ge(load_x[t].sem, 16 if 0 < t < 4 else 32)
                    for g in range(4):
                        nc.scalar.activation(bank[7][0:n, :], x_in[t % 2][0:n, g * 512:(g + 1) * 512], ACT.Square,
                                             accum_out=stats[0:n, g:g + 1]).then_inc(a_ss.sem, 1)
                        act.wait_ge(a_ss.sem, a_ss.next(i))
                    act.wait_ge(a_xs.sem, 2 * t + 1)
                    nc.scalar.activation(stats[0:n, 5:6], stats[0:n, 4:5], ACT.Sqrt, scale=1.0 / D, bias=tiny[0:n, 0:1]).then_inc(a_sqrt.sem, 1)
                    act.wait_ge(a_sqrt.sem, a_sqrt.next(i))
                    for g in range(4):
                        act.wait_ge(a_tr.sem, 4 * t + g + 1)
                        nc.scalar.copy(act_hi[:, 4 * g:4 * g + 4, t * P:t * P + n],
                                       bank[g].rearrange("p (k n) -> p k n", k=4)[:, :, 0:n]).then_inc(a_hi.sem, 1)
                        act.wait_ge(a_hi.sem, a_hi.next(i))

            @block.vector
            def _(dve):
                mine, i = v_order, 0
                dve.memset(tiny[:, 0:1], 1e-6).then_inc(mine.sem, 1)
                dve.wait_ge(mine.sem, mine.next(i))
                dve.memset(tiny[:, 1:2], 64e-5).then_inc(mine.sem, 1)
                dve.wait_ge(mine.sem, mine.next(i))
                dve.memset(tiny[:, 2:3], 1.0).then_inc(a_eps.sem, 1)
                dve.wait_ge(a_eps.sem, a_eps.next(i))
                for t in range(5):
                    n, x = rows_of[t], x_in[t % 2]
                    dve.wait_ge(a_ss.sem, 4 * t + 4)
                    dve.tensor_reduce(stats[0:n, 4:5], stats[0:n, 0:4], mybir.AxisListType.X, ADD).then_inc(a_xs.sem, 1)
                    dve.wait_ge(a_xs.sem, a_xs.next(i))
                    dve.wait_ge(a_sqrt.sem, t + 1)
                    dve.reciprocal(stats[0:n, 6:7], stats[0:n, 5:6]).then_inc(mine.sem, 1)
                    dve.wait_ge(mine.sem, mine.next(i))
                    if t == 0:
                        dve.wait_ge(load_n.sem, 16)
                    dve.scalar_tensor_tensor(out=x[0:n, :], in0=x[0:n, :], scalar=stats[0:n, 6:7], in1=norm_row[0:n, :],
                                             op0=MUL, op1=MUL).then_inc(a_xs.sem, 1)
                    dve.wait_ge(a_xs.sem, a_xs.next(i))
                    for g in range(4):
                        dve.wait_ge(a_hi.sem, 4 * t + g + 1)
                        dve.tensor_tensor(act_lo[:, 4 * g:4 * g + 4, t * P:t * P + n],
                                          bank[g].rearrange("p (k n) -> p k n", k=4)[:, :, 0:n],
                                          act_hi[:, 4 * g:4 * g + 4, t * P:t * P + n].bitcast(F32), SUB).then_inc(a_lo.sem, 1)
                        dve.wait_ge(a_lo.sem, a_lo.next(i))
                for n in range(5):
                    dve.wait_ge(a_par.sem, n + 1)
                    w = [P, 64, P, P, P][n]
                    out = params[:, n * P:n * P + w] if n < 2 else shift_in[:, (n - 2) * P:(n - 1) * P]
                    dve.tensor_copy(out, bank[4 + n % 3][:, 0:w]).then_inc(a_parc.sem, 1)
                    dve.wait_ge(a_parc.sem, a_parc.next(i))
                dve.tensor_copy(shift_in[0:LORA, 384:400], params[0:LORA, 176:192]).then_inc(mine.sem, 1)
                dve.wait_ge(mine.sem, mine.next(i))
                dve.tensor_scalar(derived[:, 0:32], params[:, W0:W0 + 32], 0.5, None, MUL).then_inc(mine.sem, 1)
                dve.wait_ge(mine.sem, mine.next(i))
                dve.tensor_scalar(derived[:, 32:48], params[:, K_A:K_A + 16], -1.0, 1.0, MUL, ADD).then_inc(mine.sem, 1)
                dve.wait_ge(mine.sem, mine.next(i))

            @block.tensor
            def _(pe):
                pe.wait_ge(a_ones.sem, 1)
                for t in range(5):
                    n = rows_of[t]
                    pe.wait_ge(a_xs.sem, 2 * t + 2)
                    for g in range(4):
                        if t:
                            pe.wait_ge(a_lo.sem, 4 * (t - 1) + g + 1)
                        for k in range(4):
                            mm = pe.transpose(bank[g][:, k * P:k * P + n], x_in[t % 2][0:n, (4 * g + k) * P:(4 * g + k + 1) * P],
                                              ident[0:n, 0:n])
                        mm.then_inc(a_tr.sem, 1)
                pe.wait_ge(load_c.sem, load_c.total)
                for n in range(5):
                    w = [P, 64, P, P, P][n]
                    if n >= 3:
                        pe.wait_ge(a_parc.sem, n - 2)
                    pe.transpose(bank[4 + n % 3][:, 0:w], prow[0:w, n, :], ident[0:w, 0:w]).then_inc(a_par.sem, 1)

        class Projection:

            def __init__(self, name, per):
                self.loaded = [sig(f"{name}_loaded{n}", 16 * per) for n in range(2)]
                self.hi, self.lo = sig(f"{name}_w_hi", 2 * per), sig(f"{name}_w_lo", 2 * per)
                self.half, self.evacuated = sig(f"{name}_half_done", 2 * per), sig(f"{name}_evacuated", 2 * per)
                self.lo.bias, self.half.bias, self.evacuated.bias = 2, 3, 2

            def load(self, sp, i, t, source, width=P):
                for half in range(2):
                    sp.wait_ge(self.lo.sem, self.lo.at(i, 2 * t - 1 + half))
                    sp.sem_inc(waited.sem, 1)
                    sp.dma_start(raw[half][:, :, 0:width], source(half).rearrange("(k p) c -> p k c", p=P)).then_inc(
                        self.loaded[half].sem, 16)

            def split_hi(self, eng, i, mine, t, width=P):
                for half in range(2):
                    eng.wait_ge(self.loaded[half].sem, self.loaded[half].at(i, 16 * (t + 1)))
                    eng.wait_ge(self.half.sem, self.half.at(i, 2 * (t - 1)))
                    ks = slice(half * KT // 2, (half + 1) * KT // 2)
                    self.hi.count = 2 * t + half
                    nc.scalar.copy(w_hi[t % 2][:, ks, 0:width], raw[half][:, :, 0:width]).then_inc(self.hi.sem, 1)
                    eng.wait_ge(self.hi.sem, self.hi.next(i))

            def split_lo(self, eng, i, mine, t, width=P):
                for half in range(2):
                    eng.wait_ge(self.hi.sem, self.hi.at(i, 2 * t + half + 1))
                    ks = slice(half * KT // 2, (half + 1) * KT // 2)
                    self.lo.count = 2 * t + half
                    eng.tensor_tensor(w_lo[t % 2][:, ks, 0:width], raw[half][:, :, 0:width],
                                           w_hi[t % 2][:, ks, 0:width].bitcast(F32), SUB).then_inc(self.lo.sem, 1)
                    eng.wait_ge(self.lo.sem, self.lo.next(i))

            def steps(self, pe, i, t, width=P, first=0, tokens=HALF):
                for half in range(2):
                    cols = slice(first + half * tokens, first + (half + 1) * tokens)
                    for k in range(KT):
                        if k == 0:
                            pe.wait_ge(self.lo.sem, self.lo.at(i, 2 * t + 2))
                            pe.wait_ge(self.evacuated.sem, self.evacuated.at(i, 2 * t - 1 + half))
                        hi, lo = w_hi[t % 2][:, k, 0:width], w_lo[t % 2][:, k, 0:width]
                        out = bank[half][0:width, 0:tokens]
                        pe.matmul(out, hi, act_hi[:, k, cols], start=(k == 0), stop=False)
                        pe.matmul(out, hi, act_lo[:, k, cols], start=False, stop=False)
                        mm = pe.matmul(out, lo, act_hi[:, k, cols], start=False, stop=(k == KT - 1))
                        if k == KT - 1:
                            mm.then_inc(self.half.sem, 1)
                        yield

            def whole(self, pe, i, t, width=P):
                for _ in self.steps(pe, i, t, width):
                    pass

        def shift_buffers(z):
            return z[:, 1 + TP:ZW].rearrange("p (s t) -> p s t", s=NSEQ)

        def to_shift_buffer(eng, i, mine, proj, t, z, n=P):
            proj.evacuated.count = 2 * t
            eng.wait_ge(proj.half.sem, proj.half.at(i, 2 * t + 1))
            nc.scalar.copy(z[0:n, 1:1 + HALF], bank[0][0:n, 0:HALF]).then_inc(proj.evacuated.sem, 1)
            eng.wait_ge(proj.evacuated.sem, proj.evacuated.next(i))
            eng.wait_ge(proj.half.sem, proj.half.at(i, 2 * t + 2))
            nc.scalar.copy(z[0:n, 1 + HALF:1 + TP], bank[1][0:n, 0:TP - HALF]).then_inc(mine.sem, 1)
            eng.wait_ge(mine.sem, mine.next(i))
            nc.scalar.copy(shift_buffers(z)[0:n, :, 1:], bank[1][0:n, TP - HALF:HALF].rearrange("p (s t) -> p s t", s=NSEQ)).then_inc(proj.evacuated.sem, 1)
            eng.wait_ge(proj.evacuated.sem, proj.evacuated.next(i))

        def token_shift(eng, i, mine, z, out, mu, n=P, done=None, scratch=None):
            z5 = shift_buffers(z)
            eng.tensor_tensor(scratch[0:n, 0:TP], z[0:n, 0:TP], z[0:n, 1:1 + TP], SUB).then_inc(mine.sem, 1)
            eng.wait_ge(mine.sem, mine.next(i))
            eng.tensor_tensor(seqs(scratch)[0:n], z5[0:n, :, 0:TS], z5[0:n, :, 1:], SUB).then_inc(mine.sem, 1)
            eng.wait_ge(mine.sem, mine.next(i))
            eng.scalar_tensor_tensor(out=out[0:n, 0:TP], in0=scratch[0:n, 0:TP], scalar=mu, in1=z[0:n, 1:1 + TP],
                                          op0=MUL, op1=ADD).then_inc(mine.sem, 1)
            eng.wait_ge(mine.sem, mine.next(i))
            signal = done or mine
            eng.scalar_tensor_tensor(out=seqs(out)[0:n], in0=seqs(scratch)[0:n], scalar=mu, in1=z5[0:n, :, 1:],
                                          op0=MUL, op1=ADD).then_inc(signal.sem, 1)
            eng.wait_ge(signal.sem, signal.next(i))

        ar = Arena()
        gate_low = ar(T)[0:GLORA]
        zb_ = [ar(ZW) for _ in range(2)]
        scratch = ar(T)
        pb = Projection("b", 3)
        v_order, s_order, g_order = sig("b_vector"), sig("b_scalar"), sig("b_pool")
        seeded, shifted, saved = sig("b_seeded"), sig("b_shifted"), sig("b_saved")
        widths = [LORA, LORA, GLORA]
        with nc.Block() as block:
            @block.sync
            def _(sp):
                sp.sem_inc(pb.lo.sem, 2)
                for t, col in enumerate((3 * D, 3 * D + LORA, COL_GLO)):
                    pb.load(sp, 0, t, lambda h: w_in[0, h * D // 2:(h + 1) * D // 2, col:col + widths[t]], widths[t])

            @block.gpsimd
            def _(pool):
                mine, i = g_order, 0
                for t in range(2):
                    pool.memset(zb_[t][:, 0:1], 0.0).then_inc(mine.sem, 1)
                    pool.wait_ge(mine.sem, mine.next(i))
                    pool.tensor_copy(shift_buffers(zb_[t])[0:LORA, :, 0],
                                     shift_in[0:LORA, 384:400].rearrange("p (s j) -> p j s", j=2)[:, t, :]).then_inc(seeded.sem, 1)
                    pool.wait_ge(seeded.sem, seeded.next(i))
                for t in range(2):
                    pool.wait_ge(pb.evacuated.sem, pb.evacuated.at(i, 2 * t + 2))
                    pool.tensor_copy(shift_out[0:LORA, 48 + t, 0:1], zb_[t][0:LORA, TP:TP + 1]).then_inc(mine.sem, 1)
                    pool.wait_ge(mine.sem, mine.next(i))
                    pool.tensor_copy(shift_out[0:LORA, 48 + t, 1:9], shift_buffers(zb_[t])[0:LORA, :, TS]).then_inc(saved.sem, 1)
                    pool.wait_ge(saved.sem, saved.next(i))

            @block.scalar
            def _(act):
                mine, i = s_order, 0
                act.sem_inc(pb.half.sem, 3)
                for t in range(2):
                    pb.split_hi(act, i, mine, t, widths[t])
                for t in range(2):
                    to_shift_buffer(act, i, mine, pb, t, zb_[t], LORA)
                    if t == 0:
                        pb.split_hi(act, i, mine, 2, widths[2])
                act.wait_ge(shifted.sem, shifted.at(i, 1))
                nc.scalar.activation(lora[0][:, :], lora[0][:, :], ACT.Tanh).then_inc(mine.sem, 1)
                act.wait_ge(mine.sem, mine.next(i))
                for half in range(2):
                    act.wait_ge(pb.half.sem, pb.half.at(i, 2 * (2) + half + 1))
                    nc.scalar.copy(gate_low[:, half * HALF:(half + 1) * HALF], bank[half][0:GLORA, 0:HALF]).then_inc(pb.evacuated.sem, 1)
                    act.wait_ge(pb.evacuated.sem, pb.evacuated.next(i))

            @block.vector
            def _(dve):
                mine, i = v_order, 0
                for t in range(3):
                    pb.split_lo(dve, i, mine, t, widths[t])
                for t in range(2):
                    dve.wait_ge(seeded.sem, seeded.at(i, t + 1))
                    dve.wait_ge(pb.evacuated.sem, pb.evacuated.at(i, 2 * t + 2))
                    token_shift(dve, i, mine, zb_[t], lora[t], params[0:LORA, MU_LO + t:MU_LO + t + 1], LORA, shifted, scratch)

            @block.tensor
            def _(pe):
                pe.sem_inc(pb.evacuated.sem, 2)
                for t in range(3):
                    pb.whole(pe, 0, t, widths[t])

        ar = Arena()
        gate_low = ar(T)[0:GLORA]
        k_g, q_g = [ar(T) for _ in range(2)], [ar(T) for _ in range(2)]
        ar.at = T
        o_g = [ar(T) for _ in range(4)]
        v_b, b_g = [ar(T) for _ in range(2)], [ar(T) for _ in range(2)]
        ar.at -= 4 * T
        gz = [ar(T) for _ in range(4)]
        v_rows = ar(NC, BV)
        qk = [ar(T) for _ in range(2)]
        exp_ = [ar(T) for _ in range(2)]
        att = ar(NC, C)
        q_s = exp_
        kd_rows = ar(NC, BK_)
        kd_seq = ar(BK_)
        gstate = [ar(2, BV) for _ in range(2)]
        sstate = [ar(2, BV) for _ in range(3)]
        q_tail = [ar(LAST) for _ in range(2)]
        ends = ar(2, NC + NSEQ)
        level_mask = ar(7, C)
        member_c = ar(NSEQ)
        ones = ar(P)
        gk_w = ar(BK_)
        LEVELS = (1, 2, 4, 8, 16, 32, 64)
        TILES = 12
        per = dict(v=DCV, s=DCS, g=DCG)
        own_signals = []

        def own(name, per=0):
            own_signals.append(Signal(scope, nc, name, per))
            return own_signals[-1]
        scope = ctx.enter_context(ExitStack())
        pc = Projection("c", TILES)
        v_order, s_order, g_order = own("c_vector", per["v"]), own("c_scalar", per["s"]), own("c_pool", per["g"])
        turn = own("c_turn", 4)
        o_all = arena[:, T:5 * T].rearrange("p (n t) -> p n t", n=4)
        gk_done, gk_x, gk_abs, gk_exp = own("c_gk_done", 2), own("c_gk_x", 2), own("c_gk_abs", 2), own("c_gk_ln", 2)
        level_diff, level_exp, level_ready = own("c_level_diff", 12), own("c_level_exp", 12), own("c_level_ready", 6)
        level_done, level_taken = own("c_level_done", 7), own("c_level_taken", 7)
        b_exp, kd_diff, kd_exp, kd_ready, kd_turned, kd_rows_ready = (own("c_" + n, 2) for n in (
            "b_exp", "kd_diff", "kd_exp", "kd_ready", "kd_turned", "kd_rows"))
        q_s_ready, ends_ready, tails_ready = own("c_q_s", 2), own("c_ends", 2), own("c_tails", 1)
        v_turned, v_rows_ready = own("c_v_turned", 4), own("c_v_rows", 4)
        o_done, o_read, ds_done, s_ready = own("c_o_done", NC), own("c_o_read", NC), own("c_ds_done", NC), own("c_s_ready", NC)
        kd_seq_ready, o8_done, ds8_done, s8_next = (own("c_" + n, NSEQ) for n in ("kd_seq", "o8_done", "ds8_done", "s8_next"))
        gate_tanh = own("c_gate_tanh", 8)
        gate_ready = own("c_gate", 4)
        squared, sq_used, var_done, root, merged = own("c_squared", 4), own("c_square_summed", 4), own("c_var_done", 1), own("c_root", 1), own("c_merged", 4)
        load_gk = sig("c_load_gk", 16)
        load_s8 = [sig(f"c_load_state{n}", 16 * len(range(n, NSEQ, 3))) for n in range(3)]
        store_s8 = [sig(f"c_store_state{n}", 16 * len(range(n, NSEQ, 3))) for n in range(3)]
        store_ob, store_p = sig("c_store_ob", 64), sig("c_store_p", 16)
        masks = own("c_masks")

        def blocks(x, level):
            n = T if level <= TS else TP if level <= TAIL else NF * C
            return x[:, 0:n].rearrange("p (n h u) -> p n h u", h=2, u=level // 2)

        def span_ends(x):
            return ((x[:, 0:NF * C].rearrange("p (c t) -> p c t", c=NF), slice(0, NF)),
                    (x[:, NF * C:TP].unsqueeze(1), slice(NF, NC)), (seqs(x), slice(NC, NC + NSEQ)))

        def all_here(eng, i):
            eng.sem_inc(waited.sem, 1)
            eng.drain().then_inc(turn.sem, 1)
            eng.wait_ge(turn.sem, turn.at(i, 4))
            eng.sem_inc(waited.sem, 1)

        with nc.Block() as block:
            @block.sync
            def _(sp):
                sp.sem_inc(pc.lo.sem, 2)
                with sp.Fori(0, BH) as i:
                    for t in range(TILES):
                        first, step, n = ((COL_K, BK_, t), (COL_Q, BK_, t - 2), (COL_V, BV, t - 4), (COL_ZB, BV, t - 8))[
                            0 if t < 2 else 1 if t < 4 else 2 if t < 8 else 3]
                        pc.load(sp, i, t, lambda h: w_in[0, h * D // 2:(h + 1) * D // 2, ds(i * step + (first + n * P), P)])

            @block.gpsimd
            def _(pool):
                mine, i = masks, 0
                pool.memset(level_mask, 0.0).then_inc(mine.sem, 1)
                pool.wait_ge(mine.sem, mine.next(i))
                m = level_mask[0:C, 0, :]
                pool.affine_select(out=m, in_=m, compare_op=ALU.not_equal, fill=1.0, base=0, pattern=[[-1, C]], channel_multiplier=1).then_inc(mine.sem, 1)
                pool.wait_ge(mine.sem, mine.next(i))
                for n, level in enumerate(LEVELS):
                    if n:
                        m = level_mask[0:C, n, :].rearrange("p (n h u) -> p n h u", h=2, u=level // 2)[:, :, 1, :]
                        pool.memset(m, 1.0).then_inc(mine.sem, 1)
                        pool.wait_ge(mine.sem, mine.next(i))
                        for sign, base in ((1, 0), (-1, level // 2 - 1)):
                            pool.affine_select(out=m, in_=m, compare_op=ALU.is_ge, fill=0.0, base=base,
                                               pattern=[[-sign * level, C // level], [0, level // 2]], channel_multiplier=sign).then_inc(mine.sem, 1)
                            pool.wait_ge(mine.sem, mine.next(i))
                pool.memset(member_c, 1.0).then_inc(mine.sem, 1)
                pool.wait_ge(mine.sem, mine.next(i))
                for sign, base in ((1, -TAIL), (-1, TAIL + TS - 1)):
                    pool.affine_select(out=member_c[0:C], in_=member_c[0:C], compare_op=ALU.is_ge, fill=0.0, base=base,
                                       pattern=[[-sign * TS, NSEQ]], channel_multiplier=sign).then_inc(mine.sem, 1)
                    pool.wait_ge(mine.sem, mine.next(i))
                pool.memset(ones, 1.0).then_inc(mine.sem, 1)
                pool.wait_ge(mine.sem, mine.next(i))
                pool.memset(v_rows[C:P], 0.0).then_inc(mine.sem, 1)
                pool.wait_ge(mine.sem, mine.next(i))
                pool.memset(v_rows[0:C, NF, :], 0.0).then_inc(mine.sem, 1)
                pool.wait_ge(mine.sem, mine.next(i))
                pool.memset(att, 0.0).then_inc(mine.sem, 1)
                pool.wait_ge(mine.sem, mine.next(i))
                pool.memset(tiny[:, 3:4], 16e-6).then_inc(mine.sem, 1)
                pool.wait_ge(mine.sem, mine.next(i))
                for n in range(2):
                    pool.memset(q_tail[n], 0.0).then_inc(mine.sem, 1)
                    pool.wait_ge(mine.sem, mine.next(i))
                with pool.Fori(0, BH) as i:
                    mine = g_order
                    all_here(pool, i)
                    pool.dma_start(gk_w[0:GLORA, :], gla_gk_w2[0, :, ds(i * BK_, BK_)]).then_inc(load_gk.sem, 16)

                    def load_state(s):
                        pool.dma_start(sstate[s % 3], state_gla[0, s, ds(i, 1)].rearrange("h (n k) v -> k (h n) v", n=2)).then_inc(
                            load_s8[s % 3].sem, 16)
                    for s in range(3):
                        load_state(s)
                    for n in range(2):
                        pool.wait_ge(q_s_ready.sem, q_s_ready.at(i, n + 1))
                        pool.sem_inc(waited.sem, 1)
                        signal = tails_ready if n else mine
                        pool.tensor_copy(q_tail[n][:, 0:TAIL], q_s[n][:, NF * C:TP]).then_inc(signal.sem, 1)
                        pool.wait_ge(signal.sem, signal.next(i))
                        pool.sem_inc(waited.sem, 1)
                    for s in range(NSEQ):
                        pool.wait_ge(s8_next.sem, s8_next.at(i, s + 1))
                        pool.sem_inc(waited.sem, 1)
                        pool.dma_start(s_gla[0, s, ds(i, 1)].rearrange("h (n k) v -> k (h n) v", n=2), sstate[s % 3]).then_inc(
                            store_s8[s % 3].sem, 16)
                        if 1 <= s < NSEQ - 2:
                            pool.wait_ge(store_s8[(s - 1) % 3].sem, store_s8[(s - 1) % 3].at(i, 16 * ((s - 1) // 3 + 1)))
                            pool.sem_inc(waited.sem, 1)
                            load_state(s + 2)
                    pool.wait_ge(s_ready.sem, s_ready.at(i, NC))
                    pool.sem_inc(waited.sem, 1)
                    pool.dma_start(p_gla[0, 0, ds(i, 1)].rearrange("h (n k) v -> k (h n) v", n=2), gstate[NF % 2]).then_inc(store_p.sem, 16)
                    for n in range(4):
                        pool.wait_ge(merged.sem, merged.at(i, n + 1))
                        pool.sem_inc(waited.sem, 1)
                        pool.dma_start(ob_dram[ds(4 * i + n, 1)].rearrange("a p t -> (a p) t"), o_g[n]).then_inc(store_ob.sem, 16)
                    pool.wait_ge(store_ob.sem, store_ob.at(i, 64))
                    pool.sem_inc(waited.sem, 1)
                    pool.wait_ge(store_p.sem, store_p.at(i, 16))
                    pool.sem_inc(waited.sem, 1)
                    for n in range(3):
                        pool.wait_ge(store_s8[n].sem, store_s8[n].at(i, store_s8[n].per))
                        pool.sem_inc(waited.sem, 1)
                    mine.close()

            @block.scalar
            def _(act):
                act.sem_inc(pc.half.sem, 3)
                with act.Fori(0, BH) as i:
                    mine = s_order
                    activation, copy = nc.scalar.activation, nc.scalar.copy
                    pc.split_hi(act, i, mine, 0)
                    all_here(act, i)
                    for n in range(2):
                        act.wait_ge(gk_done.sem, gk_done.at(i, n + 1))
                        for half in range(2):
                            act.sem_inc(waited.sem, 1)
                            signal = gk_x if half else mine
                            activation(b_g[n][:, half * HALF:(half + 1) * HALF], bank[4 + 2 * n + half][:, 0:HALF], ACT.Identity,
                                       bias=params[:, ds(2 * i + (GK_B + n), 1)]).then_inc(signal.sem, 1)
                            act.wait_ge(signal.sem, signal.next(i))
                    for n in range(2):
                        act.wait_ge(gk_abs.sem, gk_abs.at(i, n + 1))
                        activation(qk[n], qk[n], ACT.Exp, scale=-1.0).then_inc(mine.sem, 1)
                        act.wait_ge(mine.sem, mine.next(i))
                    for n in range(2):
                        activation(qk[n], qk[n], ACT.Ln, bias=tiny[:, 2:3]).then_inc(gk_exp.sem, 1)
                        act.wait_ge(gk_exp.sem, gk_exp.next(i))
                    for t in range(8):
                        pc.split_hi(act, i, mine, t + 1)
                        for half in range(2):
                            level = 2 * (t - 4) + half
                            if 1 <= level <= 6:
                                for n in range(2):
                                    act.wait_ge(level_diff.sem, level_diff.at(i, 2 * level + n - 1))
                                    e = blocks(exp_[n], LEVELS[level])
                                    activation(e[:, :, 0, :], e[:, :, 0, :], ACT.Exp, scale=-1.0 / 16).then_inc(mine.sem, 1)
                                    act.wait_ge(mine.sem, mine.next(i))
                                    activation(e[:, :, 1, :], e[:, :, 1, :], ACT.Exp, scale=1.0 / 16).then_inc(level_exp.sem, 1)
                                    act.wait_ge(level_exp.sem, level_exp.next(i))
                            if t >= 6:
                                act.wait_ge(v_turned.sem, v_turned.at(i, t - 5))
                            act.wait_ge(pc.half.sem, pc.half.at(i, 2 * t + half + 1))
                            src, cols = bank[half][:, 0:HALF], slice(half * HALF, (half + 1) * HALF)
                            if t in (2, 3):
                                nc.scalar.mul(q_g[t - 2][:, cols], src, BK_ ** -0.5).then_inc(pc.evacuated.sem, 1)
                                act.wait_ge(pc.evacuated.sem, pc.evacuated.next(i))
                            else:
                                copy((k_g[t] if t < 2 else v_b[t % 2])[:, cols], src).then_inc(pc.evacuated.sem, 1)
                                act.wait_ge(pc.evacuated.sem, pc.evacuated.next(i))
                    for n in range(2):
                        act.wait_ge(level_taken.sem, level_taken.at(i, 6))
                        act.wait_ge(level_ready.sem, level_ready.at(i, 6))
                        activation(exp_[n], b_g[n], ACT.Exp, scale=1.0 / 16).then_inc(b_exp.sem, 1)
                        act.wait_ge(b_exp.sem, b_exp.next(i))
                        for tokens, at in span_ends(b_g[n]):
                            signal = ends_ready if at.stop == NC + NSEQ else mine
                            activation(ends[:, n, at], tokens[:, :, tokens.shape[2] - 1], ACT.Exp, scale=1.0 / 16).then_inc(signal.sem, 1)
                            act.wait_ge(signal.sem, signal.next(i))
                    for n in range(2):
                        act.wait_ge(kd_diff.sem, kd_diff.at(i, n + 1))
                        activation(qk[n], qk[n], ACT.Exp, scale=1.0 / 16).then_inc(kd_exp.sem, 1)
                        act.wait_ge(kd_exp.sem, kd_exp.next(i))
                    for n in range(2):
                        act.wait_ge(kd_turned.sem, kd_turned.at(i, n + 1))
                        for b in range(3):
                            chunks, w = (slice(4 * b, 4 * b + 4), C) if b < 2 else (slice(NF, NC), LAST)
                            signal = kd_rows_ready if b == 2 else mine
                            copy(kd_rows[0:w, chunks, n * P:(n + 1) * P],
                                 bank[4 + b][0:w, 0:(chunks.stop - chunks.start) * P].rearrange("p (c k) -> p c k", k=P)).then_inc(signal.sem, 1)
                            act.wait_ge(signal.sem, signal.next(i))
                    for c in range(NC):
                        act.wait_ge(o_done.sem, o_done.at(i, c + 1))
                        if c < NF:
                            copy(o_all[:, :, c * C:(c + 1) * C], bank[2 + c % 2][:, 0:4 * C].rearrange("p (n t) -> p n t", n=4)).then_inc(o_read.sem, 1)
                            act.wait_ge(o_read.sem, o_read.next(i))
                        else:
                            for b in range(2):
                                signal = o_read if b else mine
                                copy(o_all[:, 2 * b:2 * b + 2, NF * C:T], psum[:, 2 + 4 * b:4 + 4 * b, 0:LAST]).then_inc(signal.sem, 1)
                                act.wait_ge(signal.sem, signal.next(i))
                        if c % 2:
                            n = c // 2
                            if n < 3:
                                pc.split_hi(act, i, mine, 9 + n)
                            if n:
                                act.wait_ge(gate_ready.sem, gate_ready.at(i, n))
                            for half in range(2):
                                act.wait_ge(pc.half.sem, pc.half.at(i, 2 * (8 + n) + half + 1))
                                activation(qk[0][:, half * HALF:(half + 1) * HALF], bank[half][:, 0:HALF], ACT.Tanh, scale=0.5).then_inc(gate_tanh.sem, 1)
                                act.wait_ge(gate_tanh.sem, gate_tanh.next(i))
                    act.wait_ge(gate_ready.sem, gate_ready.at(i, 4))
                    for n in range(4):
                        if n >= 2:
                            act.wait_ge(sq_used.sem, sq_used.at(i, n - 1))
                        activation(qk[n % 2], o_g[n], ACT.Square).then_inc(squared.sem, 1)
                        act.wait_ge(squared.sem, squared.next(i))
                    act.wait_ge(sq_used.sem, sq_used.at(i, 4))
                    for half in range(2):
                        signal = root if half else mine
                        activation(exp_[0][:, half * HALF:(half + 1) * HALF], bank[2 + half][:, 0:HALF], ACT.Sqrt,
                                   scale=16.0 / BV, bias=tiny[:, 3:4]).then_inc(signal.sem, 1)
                        act.wait_ge(signal.sem, signal.next(i))
                    mine.close()

            @block.vector
            def _(dve):
                with dve.Fori(0, BH) as i:
                    mine = v_order
                    tt, stt = dve.tensor_tensor, dve.scalar_tensor_tensor
                    pc.split_lo(dve, i, mine, 0)
                    all_here(dve, i)
                    for n in range(2):
                        dve.wait_ge(gk_x.sem, gk_x.at(i, n + 1))
                        stt(out=qk[n], in0=b_g[n], scalar=-1.0, in1=b_g[n], op0=MUL, op1=MAX).then_inc(gk_abs.sem, 1)
                        dve.wait_ge(gk_abs.sem, gk_abs.next(i))
                    for n in range(2):
                        dve.wait_ge(gk_exp.sem, gk_exp.at(i, n + 1))
                        stt(out=exp_[n], in0=b_g[n], scalar=0.0, in1=qk[n], op0=MIN, op1=SUB).then_inc(mine.sem, 1)
                        dve.wait_ge(mine.sem, mine.next(i))
                        dve.tensor_tensor_scan(b_g[n], chunk_start[:, :], exp_[n], 0.0, MUL, ADD).then_inc(mine.sem, 1)
                        dve.wait_ge(mine.sem, mine.next(i))

                    def take(level):
                        dve.wait_ge(level_done.sem, level_done.at(i, level + 1))
                        m = level_mask[0:C, level, :]
                        w = LAST if LEVELS[level] <= TS else TAIL if LEVELS[level] <= TAIL else 0
                        dve.sem_inc(waited.sem, 1)
                        signal = mine if w else level_taken
                        dve.copy_predicated(att[0:C, 0:NF, :], bc(m, NF).bitcast(I32), bank[2][0:C, :].rearrange("p (c t) -> p c t", c=NF)).then_inc(signal.sem, 1)
                        dve.wait_ge(signal.sem, signal.next(i))
                        if w:
                            dve.sem_inc(waited.sem, 1)
                            dve.copy_predicated(att[0:w, NF, 0:w], m[0:w, 0:w].bitcast(I32), bank[3][0:w, 0:w]).then_inc(level_taken.sem, 1)
                            dve.wait_ge(level_taken.sem, level_taken.next(i))

                    def rows(n):
                        dve.wait_ge(v_turned.sem, v_turned.at(i, n + 1))
                        for b in range(3):
                            chunks, w = (slice(4 * b, 4 * b + 4), C) if b < 2 else (slice(NF, NC), LAST)
                            signal = v_rows_ready if b == 2 else mine
                            dve.tensor_copy(v_rows[0:w, chunks, n * P:(n + 1) * P],
                                            bank[4 + b][0:w, 0:(chunks.stop - chunks.start) * P].rearrange("p (c k) -> p c k", k=P)).then_inc(signal.sem, 1)
                            dve.wait_ge(signal.sem, signal.next(i))
                    for t in range(8):
                        pc.split_lo(dve, i, mine, t + 1)
                        if t < 4:
                            continue
                        if t == 4:
                            dve.wait_ge(pc.evacuated.sem, pc.evacuated.at(i, 8))
                        for half in range(2):
                            level = 2 * (t - 4) + half
                            if 1 <= level <= 6:
                                L = LEVELS[level]
                                for n in range(2):
                                    b = blocks(b_g[n], L).rearrange("p n h u -> p n (h u)")
                                    mid = b[:, :, L // 2 - 1:L // 2]
                                    tt(blocks(exp_[n], L).rearrange("p n h u -> p n (h u)"), b, mid.to_broadcast(list(b.shape)), SUB).then_inc(level_diff.sem, 1)
                                    dve.wait_ge(level_diff.sem, level_diff.next(i))
                                take(level - 1)
                                for n in range(2):
                                    dve.wait_ge(level_exp.sem, level_exp.at(i, 2 * level + n - 1))
                                    for h, x in enumerate((k_g[n], q_g[n])):
                                        signal = level_ready if n and h else mine
                                        tt(blocks(qk[n], L)[:, :, h, :], blocks(exp_[n], L)[:, :, h, :], blocks(x, L)[:, :, h, :], MUL).then_inc(signal.sem, 1)
                                        dve.wait_ge(signal.sem, signal.next(i))
                            if half and t > 4:
                                rows(t - 5)
                    take(6)
                    rows(3)
                    for n in range(2):
                        dve.wait_ge(b_exp.sem, b_exp.at(i, n + 1))
                        tt(q_s[n], exp_[n], q_g[n], MUL).then_inc(q_s_ready.sem, 1)
                        dve.wait_ge(q_s_ready.sem, q_s_ready.next(i))
                        for (out, _), (b, at) in zip(span_ends(qk[n]), span_ends(b_g[n])):
                            w = b.shape[2]
                            signal = kd_diff if at.stop == NC + NSEQ else mine
                            tt(out, b[:, :, w - 1:w].to_broadcast(list(b.shape)), b, SUB).then_inc(signal.sem, 1)
                            dve.wait_ge(signal.sem, signal.next(i))
                    for n in range(2):
                        dve.wait_ge(kd_exp.sem, kd_exp.at(i, n + 1))
                        tt(qk[n], qk[n], k_g[n], MUL).then_inc(kd_ready.sem, 1)
                        dve.wait_ge(kd_ready.sem, kd_ready.next(i))
                    dve.wait_ge(ends_ready.sem, ends_ready.at(i, 2))
                    for c in range(NC):
                        b = 4 + 2 * (c % 2)
                        dve.wait_ge(ds_done.sem, ds_done.at(i, c + 1))
                        if c:
                            dve.wait_ge(o_done.sem, o_done.at(i, c))
                        for n in range(2):
                            if c:
                                signal = s_ready if n else mine
                                stt(out=gstate[c % 2][:, n, :], in0=gstate[(c - 1) % 2][:, n, :], scalar=ends[:, n, c:c + 1],
                                    in1=bank[b + n], op0=MUL, op1=ADD).then_inc(signal.sem, 1)
                                dve.wait_ge(signal.sem, signal.next(i))
                            else:
                                signal = s_ready if n else mine
                                dve.tensor_copy(gstate[0][:, n, :], bank[b + n]).then_inc(signal.sem, 1)
                                dve.wait_ge(signal.sem, signal.next(i))
                        if c % 2:
                            n = c // 2
                            if n < 3:
                                pc.split_lo(dve, i, mine, 9 + n)
                            for half in range(2):
                                dve.wait_ge(gate_tanh.sem, gate_tanh.at(i, 2 * n + half + 1))
                                cols = slice(half * HALF, (half + 1) * HALF)
                                stt(out=gz[n][:, cols], in0=qk[0][:, cols], scalar=1.0, in1=bank[half][:, 0:HALF], op0=ADD, op1=MUL).then_inc(pc.evacuated.sem, 1)
                                dve.wait_ge(pc.evacuated.sem, pc.evacuated.next(i))
                            dve.tensor_scalar(gz[n], gz[n], params[:, NORM_W + n:NORM_W + n + 1], None, MUL).then_inc(gate_ready.sem, 1)
                            dve.wait_ge(gate_ready.sem, gate_ready.next(i))
                    for s in range(NSEQ):
                        if s:
                            dve.wait_ge(ds8_done.sem, ds8_done.at(i, s))
                        dve.tensor_scalar(kd_seq[0:LAST], kd_rows[0:LAST, NF, :], member_c[0:LAST, s:s + 1], None, MUL).then_inc(kd_seq_ready.sem, 1)
                        dve.wait_ge(kd_seq_ready.sem, kd_seq_ready.next(i))
                        dve.wait_ge(ds8_done.sem, ds8_done.at(i, s + 1))
                        for n in range(2):
                            signal = s8_next if n else mine
                            stt(out=sstate[s % 3][:, n, :], in0=sstate[s % 3][:, n, :], scalar=ends[:, n, NC + s:NC + s + 1],
                                in1=bank[4 + n], op0=MUL, op1=ADD).then_inc(signal.sem, 1)
                            dve.wait_ge(signal.sem, signal.next(i))
                    dve.wait_ge(root.sem, root.at(i, 1))
                    dve.reciprocal(exp_[0], exp_[0]).then_inc(mine.sem, 1)
                    dve.wait_ge(mine.sem, mine.next(i))
                    for n in range(4):
                        tt(o_g[n], o_g[n], exp_[0], MUL).then_inc(mine.sem, 1)
                        dve.wait_ge(mine.sem, mine.next(i))
                        tt(o_g[n], o_g[n], gz[n], MUL).then_inc(merged.sem, 1)
                        dve.wait_ge(merged.sem, merged.next(i))
                    mine.close()

            @block.tensor
            def _(pe):
                pe.wait_ge(masks.sem, masks.count)
                pe.sem_inc(pc.evacuated.sem, 2)
                with pe.Fori(0, BH) as i:
                    all_here(pe, i)
                    mm, tr = pe.matmul, pe.transpose
                    pe.wait_ge(load_gk.sem, load_gk.at(i, 16))
                    pe.sem_inc(waited.sem, 1)
                    for n in range(2):
                        for half in range(2):
                            m = mm(bank[4 + 2 * n + half][:, 0:HALF], gk_w[0:GLORA, n * P:(n + 1) * P], gate_low[:, half * HALF:(half + 1) * HALF],
                                   start=True, stop=True)
                        m.then_inc(gk_done.sem, 1)

                    def gram_level(level):
                        L = LEVELS[level]
                        if level == 0:
                            pe.wait_ge(pc.evacuated.sem, pc.evacuated.at(i, 8))
                            pe.sem_inc(waited.sem, 1)
                        else:
                            pe.wait_ge(level_taken.sem, level_taken.at(i, level))
                            pe.sem_inc(waited.sem, 1)
                            pe.wait_ge(level_ready.sem, level_ready.at(i, level))
                            pe.sem_inc(waited.sem, 1)
                        for c in range(NC):
                            w = C if c < NF else LAST if L <= TS else TAIL if L <= TAIL else 0
                            at = slice(c * C, c * C + w)
                            for n in range(2):
                                if w:
                                    left, right = (qk[n], qk[n]) if level else (k_g[n], q_g[n])
                                    m = mm(bank[2 + c // NF][0:w, c % NF * C:c % NF * C + w], left[:, at], right[:, at], start=(n == 0), stop=(n == 1))
                        m.then_inc(level_done.sem, 1)

                    def turn_rows(x, signal):
                        for c in range(NC):
                            w = C if c < NF else LAST
                            m = tr(bank[4 + c // 4][0:w, c % 4 * P:(c % 4 + 1) * P], x[:, c * C:c * C + w], ident[:, :])
                        m.then_inc(signal.sem, 1)

                    def turn_v(n):
                        pe.wait_ge(pc.evacuated.sem, pc.evacuated.at(i, 2 * (4 + n) + 2))
                        pe.sem_inc(waited.sem, 1)
                        if n:
                            pe.wait_ge(v_rows_ready.sem, v_rows_ready.at(i, n))
                            pe.sem_inc(waited.sem, 1)
                        turn_rows(v_b[n % 2], v_turned)
                    for t in range(4):
                        pc.whole(pe, i, t)
                    for t in range(4, 8):
                        fill = pc.steps(pe, i, t)
                        for _ in range(16):
                            next(fill)
                        gram_level(2 * (t - 4))
                        if t > 4:
                            turn_v(t - 5)
                        for _ in fill:
                            pass
                        if t < 7:
                            gram_level(2 * (t - 4) + 1)
                    turn_v(3)
                    pe.wait_ge(v_rows_ready.sem, v_rows_ready.at(i, 4))
                    pe.sem_inc(waited.sem, 1)
                    pe.wait_ge(kd_ready.sem, kd_ready.at(i, 1))
                    pe.sem_inc(waited.sem, 1)
                    turn_rows(qk[0], kd_turned)
                    pe.wait_ge(kd_ready.sem, kd_ready.at(i, 2))
                    pe.sem_inc(waited.sem, 1)
                    pe.wait_ge(kd_rows_ready.sem, kd_rows_ready.at(i, 1))
                    pe.sem_inc(waited.sem, 1)
                    turn_rows(qk[1], kd_turned)
                    pe.wait_ge(kd_rows_ready.sem, kd_rows_ready.at(i, 2))
                    pe.sem_inc(waited.sem, 1)
                    pe.wait_ge(level_taken.sem, level_taken.at(i, 7))
                    pe.sem_inc(waited.sem, 1)
                    pe.wait_ge(q_s_ready.sem, q_s_ready.at(i, 2))
                    pe.sem_inc(waited.sem, 1)
                    kv = lambda n: slice(n * P, (n + 1) * P)
                    for c in range(NC):
                        w = C if c < NF else TAIL
                        if c >= 2:
                            pe.wait_ge(s_ready.sem, s_ready.at(i, c - 1))
                            pe.sem_inc(waited.sem, 1)
                        for n in range(2):
                            m = mm(bank[4 + 2 * (c % 2) + n], kd_rows[0:w, c, kv(n)], v_rows[0:w, c, :], start=True, stop=True)
                        m.then_inc(ds_done.sem, 1)
                        if c:
                            pe.wait_ge(s_ready.sem, s_ready.at(i, c))
                            pe.sem_inc(waited.sem, 1)
                        if c == NF:
                            break
                        if c >= 2:
                            pe.wait_ge(o_read.sem, o_read.at(i, c - 1))
                            pe.sem_inc(waited.sem, 1)
                        for n in range(4):
                            out = bank[2 + c % 2][:, n * C:(n + 1) * C]
                            if c:
                                for k in range(2):
                                    mm(out, gstate[(c - 1) % 2][:, k, kv(n)], q_s[k][:, c * C:(c + 1) * C], start=(k == 0), stop=False)
                            m = mm(out, v_rows[:, c, kv(n)], att[:, c, :], start=(c == 0), stop=True)
                        m.then_inc(o_done.sem, 1)
                        if c % 2:
                            pc.whole(pe, i, 8 + c // 2)
                    pe.wait_ge(o_read.sem, o_read.at(i, NF))
                    pe.sem_inc(waited.sem, 1)
                    pe.wait_ge(tails_ready.sem, tails_ready.at(i, 1))
                    pe.sem_inc(waited.sem, 1)
                    o8 = [bank[b] for b in (2, 3, 6, 7)]
                    for n in range(4):
                        for k in range(2):
                            mm(o8[n][:, 0:LAST], gstate[(NF - 1) % 2][:, k, kv(n)], q_tail[k], start=(k == 0), stop=False, skip_group_check=True)
                    for s in range(NSEQ):
                        pe.wait_ge(load_s8[s % 3].sem, load_s8[s % 3].at(i, 16 * (s // 3 + 1)))
                        pe.sem_inc(waited.sem, 1)
                        for n in range(4):
                            for k in range(2):
                                m = mm(o8[n][:, TAIL + s * TS:TAIL + (s + 1) * TS], sstate[s % 3][:, k, kv(n)], q_s[k][:, TP + s * TS:TP + (s + 1) * TS],
                                       start=False, stop=False, skip_group_check=True)
                        pe.wait_ge(kd_seq_ready.sem, kd_seq_ready.at(i, s + 1))
                        pe.sem_inc(waited.sem, 1)
                        if s:
                            pe.wait_ge(s8_next.sem, s8_next.at(i, s))
                            pe.sem_inc(waited.sem, 1)
                        else:
                            pe.wait_ge(s_ready.sem, s_ready.at(i, NC))
                            pe.sem_inc(waited.sem, 1)
                        for n in range(2):
                            m = mm(bank[4 + n], kd_seq[0:LAST, kv(n)], v_rows[0:LAST, NF, :], start=True, stop=True)
                        m.then_inc(ds8_done.sem, 1)
                    for n in range(4):
                        m = mm(o8[n][:, 0:LAST], v_rows[:, NF, kv(n)], att[:, NF, 0:LAST], start=False, stop=True, skip_group_check=True)
                    m.then_inc(o_done.sem, 1)
                    for n in range(4):
                        pe.wait_ge(squared.sem, squared.at(i, n + 1))
                        pe.sem_inc(waited.sem, 1)
                        for half in range(2):
                            m = mm(bank[2 + half][:, 0:HALF], ones, qk[n % 2][:, half * HALF:(half + 1) * HALF], start=(n == 0), stop=(n == 3))
                        m.then_inc(sq_used.sem, 1)
        with nc.Block() as block:
            @block.gpsimd
            def _(pool):
                for s in own_signals:
                    pool.sem_clear(s.sem)
        scope.close()

        ar = Arena()
        z_ = [ar(ZW) for _ in range(2)]
        v_pad = ar(C + NC * C)
        early = ar.at
        k_t, r_t, cum, a_t, kk_t, exc, sq, e_t, lw = (ar(T) for _ in range(9))
        middle = ar.at
        ar.at = early
        n_d, t_d, x2, t2, t_full, inv = (ar(NC, C) for _ in range(6))
        ar.at = early
        state_out = ar(NC, P)
        assert ar.at <= middle
        ar.at = middle
        bonus, gate, y_t, tg, ob = (ar(T) for _ in range(5))
        a_r, b_k = ar(NC, P), ar(NC, P)
        gram = ar(NC, 2, P)
        state8_in = gram[:, 0:4].rearrange("p c h t -> p (c h t)").rearrange("p (s k) -> p s k", s=NSEQ)
        bk_t = ar(NC, P)
        uv = ar(NC, P)
        causal = ar(2, P)
        lower = ar(2, C)
        block16 = ar(C)
        eye2 = ar(C)
        member = ar(9)
        states = ar(NC, C)
        state_decayed, rhs = ar(C), ar(C)
        s8, s8_new = ar(NSEQ, C), ar(NSEQ, C)
        a8 = ar(640)
        uv8 = [ar(NC, C) for _ in range(2)]
        from_v = ar(NC, C)
        decays = ar(NC + NSEQ)
        lora_w = [ar(P) for _ in range(2)]
        r_tail = ar(LAST)
        a8g = a8[:, 0:NC * C].rearrange("p (g t) -> p g t", g=NC)

        pd = Projection("d", 6)
        v_order, s_order, g_order = sig("d_vector", DV), sig("d_scalar", DS), sig("d_pool", DG)
        s_first = sig("d_scalar_first")
        turn = sig("d_turn", 4)
        seeded, shifted, saved = sig("d_seeded", 3), sig("d_shifted", 3), sig("d_saved", 3)
        low_done, low_read = sig("d_low_done", 2), sig("d_low_read", 2)
        k_squared, square_sum, key_norm = sig("d_k_squared", 1), sig("d_square_sum", 1), sig("d_key_norm", 1)
        cum_ready, exps = sig("d_cum", 1), sig("d_exps", 3)
        rk_ready, rk_sum, bonus_done = sig("d_rk", 1), sig("d_rk_sum", 1), sig("d_bonus", 1)
        products, tanh_gate = sig("d_products", 1), sig("d_tanh_gate", 6)
        decays_ready, a8_ready = sig("d_decays", 1), sig("d_a8", 1)
        gram_done, gram_read, turned, turned_read = sig("d_gram_done", NC), sig("d_gram_read", NC), sig("d_turned", NC), sig("d_turned_read", NC)
        s8_turned, s8_ready = sig("d_s8_turned", 1), sig("d_s8_ready", 1)
        inv_mm, inv_a, inv_b, inv_ready = sig("d_inverse_products", 8), sig("d_inverse_scalar", 5), sig("d_inverse_vector", 11), sig("d_inverse_start", 1)
        t_done, from_v_done, from_v_read = sig("d_t_done", 1), sig("d_from_v_done", 1), sig("d_from_v_read", 1)
        rhs_done, rhs_ready, u_done, u_ready = sig("d_rhs_done", NC - 1), sig("d_rhs_ready", NC - 1), sig("d_u_done", NC), sig("d_u_ready", NC)
        y_uv, y_state, y_copied, y_ready, s_done, s_ready, decayed = sig("d_y_uv", 1), sig("d_y_state", 1), sig("d_y_copied", 1), sig("d_y_ready", 1), sig("d_s_done", NC), sig("d_s_ready", NC), sig("d_decayed", NC)
        uv8_ready = sig("d_uv8", 2)
        s8_done, s8_next = sig("d_s8_done", 1), sig("d_s8_next", 1)
        mean_done, centred, squared, var_done, root = sig("d_mean_done", 1), sig("d_centred", 1), sig("d_squared", 1), sig("d_var_done", 1), sig("d_root", 1)
        merged = sig("d_merged", 1)
        out_turned, out_read = sig("d_out_turned", 3), sig("d_out_read", 3)
        load_low, load_s8, load_ob = sig("d_load_low", 32), sig("d_load_s8", 16 * NSEQ), sig("d_load_ob", 16)
        store_m, store_s = sig("d_store_m", 16), sig("d_store_state", 16 * (NSEQ + 1))
        masks = sig("d_masks")

        def save(eng, i, mine, t):
            j = (16, 0, 32)[t]
            eng.wait_ge(pd.evacuated.sem, pd.evacuated.at(i, 2 * t + 2))
            out = shift_out[:, ds(i + j, 1), :].rearrange("p a s -> p (a s)")
            nc.gpsimd.tensor_copy(out[:, 0:1], z_[t % 2][:, TP:TP + 1]).then_inc(mine.sem, 1)
            eng.wait_ge(mine.sem, mine.next(i))
            nc.gpsimd.tensor_copy(out[:, 1:9], shift_buffers(z_[t % 2])[:, :, TS]).then_inc(saved.sem, 1)
            eng.wait_ge(saved.sem, saved.next(i))

        def chunked(ap):
            return ap[:, 0:NF * C].rearrange("p (c t) -> p c t", c=NF)

        LAST_TURN = NPAIR - 1
        MERGE_AT = 3
        TILES = (D, 0, 2 * D, COL_ZA, COL_GA, COL_GB)

        def recount():
            for s in (v_order, s_order, g_order, seeded, shifted, saved, low_read, k_squared, key_norm, cum_ready, exps, rk_ready,
                      bonus_done, products, tanh_gate, decays_ready, a8_ready, gram_read, turned_read, s8_ready, inv_a, inv_b,
                      inv_ready, from_v_read, rhs_ready, u_ready, y_copied, y_ready, s_ready, decayed, uv8_ready, s8_next, centred,
                      squared, root, merged, out_read):
                s.count = 0

        with nc.Block() as block:
            @block.sync
            def _(sp):
                sp.sem_inc(pd.lo.sem, 2)

                def load(i, t):
                    col = TILES[t % 6] + t // 6 * P
                    pd.load(sp, i, t, lambda h: w_in[0, h * D // 2:(h + 1) * D // 2, ds(i * P + col, P)])
                for t in range(3):
                    load(0, t)
                with sp.Fori(0, LAST_TURN) as i:
                    for t in range(3, 9):
                        load(i, t)
                for t in range(3, 6):
                    load(LAST_TURN, t)

            @block.gpsimd
            def _(pool):
                mine, i = masks, 0
                pool.memset(causal, 1.0).then_inc(mine.sem, 1)
                pool.wait_ge(mine.sem, mine.next(i))
                for half in range(2):
                    rows = slice(64 * half, 64 * half + 64)
                    for n in range(2):
                        m = causal[rows, n, :].rearrange("p (a t) -> p a t", a=2)
                        pool.affine_select(out=m, in_=m, compare_op=ALU.is_ge, fill=0.0, base=-1, pattern=[[1, 2], [1, C]],
                                           channel_multiplier=-1).then_inc(mine.sem, 1)
                        pool.wait_ge(mine.sem, mine.next(i))
                    for a in range(2):
                        m = causal[rows, 1, a * C:a * C + TAIL]
                        pool.affine_select(out=m, in_=m, compare_op=ALU.is_ge, fill=0.0, base=TAIL - 1, pattern=[[0, TAIL]],
                                           channel_multiplier=-1).then_inc(mine.sem, 1)
                        pool.wait_ge(mine.sem, mine.next(i))
                        m = causal[rows, 1, a * C + TAIL:(a + 1) * C].rearrange("p (g u) -> p g u", u=TS)
                        pool.affine_select(out=m, in_=m, compare_op=ALU.is_ge, fill=0.0, base=-TAIL,
                                           pattern=[[-TS, 12], [0, TS]], channel_multiplier=1).then_inc(mine.sem, 1)
                        pool.wait_ge(mine.sem, mine.next(i))
                pool.memset(lower, 1.0).then_inc(mine.sem, 1)
                pool.wait_ge(mine.sem, mine.next(i))
                pool.memset(block16, 1.0).then_inc(mine.sem, 1)
                pool.wait_ge(mine.sem, mine.next(i))
                pool.memset(eye2, 0.0).then_inc(mine.sem, 1)
                pool.wait_ge(mine.sem, mine.next(i))
                pool.memset(member, 1.0).then_inc(mine.sem, 1)
                pool.wait_ge(mine.sem, mine.next(i))
                for half in range(2):
                    rows = slice(64 * half, 64 * half + 64)
                    for n in range(2):
                        m = lower[rows, n, :]
                        pool.affine_select(out=m, in_=m, compare_op=ALU.is_ge, fill=0.0, base=-1, pattern=[[-1, C]],
                                           channel_multiplier=1).then_inc(mine.sem, 1)
                        pool.wait_ge(mine.sem, mine.next(i))
                    m = lower[rows, 1, 0:TAIL]
                    pool.affine_select(out=m, in_=m, compare_op=ALU.is_ge, fill=0.0, base=TAIL - 1, pattern=[[0, TAIL]],
                                       channel_multiplier=-1).then_inc(mine.sem, 1)
                    pool.wait_ge(mine.sem, mine.next(i))
                    m = lower[rows, 1, TAIL:C].rearrange("p (g u) -> p g u", u=TS)
                    pool.affine_select(out=m, in_=m, compare_op=ALU.is_ge, fill=0.0, base=TAIL + TS - 1,
                                       pattern=[[TS, 12], [0, TS]], channel_multiplier=-1).then_inc(mine.sem, 1)
                    pool.wait_ge(mine.sem, mine.next(i))
                    m = block16[rows, :].rearrange("p (g u) -> p g u", u=16)
                    pool.affine_select(out=m, in_=m, compare_op=ALU.is_ge, fill=0.0, base=0, pattern=[[-16, 4], [0, 16]],
                                       channel_multiplier=1).then_inc(mine.sem, 1)
                    pool.wait_ge(mine.sem, mine.next(i))
                    pool.affine_select(out=m, in_=m, compare_op=ALU.is_ge, fill=0.0, base=15, pattern=[[16, 4], [0, 16]],
                                       channel_multiplier=-1).then_inc(mine.sem, 1)
                    pool.wait_ge(mine.sem, mine.next(i))
                    m = eye2[rows, :]
                    pool.affine_select(out=m, in_=m, compare_op=ALU.not_equal, fill=1.0, base=0, pattern=[[-1, C]],
                                       channel_multiplier=1).then_inc(mine.sem, 1)
                    pool.wait_ge(mine.sem, mine.next(i))
                    m = member[rows, 0:1]
                    pool.affine_select(out=m, in_=m, compare_op=ALU.is_ge, fill=0.0, base=TAIL - 1, pattern=[[0, 1]],
                                       channel_multiplier=-1).then_inc(mine.sem, 1)
                    pool.wait_ge(mine.sem, mine.next(i))
                    m = member[rows, 1:9]
                    pool.affine_select(out=m, in_=m, compare_op=ALU.is_ge, fill=0.0, base=-TAIL, pattern=[[-TS, NSEQ]],
                                       channel_multiplier=1).then_inc(mine.sem, 1)
                    pool.wait_ge(mine.sem, mine.next(i))
                    pool.affine_select(out=m, in_=m, compare_op=ALU.is_ge, fill=0.0, base=TAIL + TS - 1,
                                       pattern=[[TS, NSEQ]], channel_multiplier=-1).then_inc(mine.sem, 1)
                    pool.wait_ge(mine.sem, mine.next(i))
                for tile in (a_r[:, NF, :], b_k[:, NF, :], v_pad, a8, r_tail, z_[0][:, 0:1], z_[1][:, 0:1]):
                    pool.memset(tile, 0.0).then_inc(mine.sem, 1)
                    pool.wait_ge(mine.sem, mine.next(i))

                def seed(eng, i, mine, t):
                    seeded.count = t if t < 6 else t - 3
                    first = (16, 0, 32)[t % 6] + t // 6
                    pool.tensor_copy(shift_buffers(z_[t % 2])[:, :, 0],
                                     shift_in[:, 0:384].rearrange("p (s j) -> p s j", j=48)[:, :, ds(i + first, 1)].rearrange(
                                         "p s j -> p (s j)")).then_inc(seeded.sem, 1)
                    eng.wait_ge(seeded.sem, seeded.next(i))

                def load_lora(at):
                    for n, w in enumerate((rwkv_w2, rwkv_a2)):
                        pool.dma_start(lora_w[n][0:LORA, :], w[0, :, at]).then_inc(load_low.sem, 16)
                load_lora(slice(0, P))
                mine, i = masks, 0
                for t in range(2):
                    seed(pool, i, mine, t)

                def turn_of(i, last=False):
                    recount()
                    mine = g_order
                    all_here(pool, i)
                    for s in range(NSEQ):
                        pool.dma_start(state8_in[0:C, s, :].rearrange("v (h k) -> v h k", h=2),
                                       state_rwkv[0, s, ds(2 * i, 2)].rearrange("h v k -> v h k")).then_inc(load_s8.sem, 16)
                    pool.dma_start(ob, ob_dram[ds(i, 1)].rearrange("a p t -> (a p) t")).then_inc(load_ob.sem, 16)
                    save(pool, i, mine, 0)
                    save(pool, i, mine, 1)
                    pool.wait_ge(shifted.sem, shifted.at(i, 1))
                    pool.sem_inc(waited.sem, 1)
                    seed(pool, i, mine, 2)
                    save(pool, i, mine, 2)
                    if not last:
                        pool.wait_ge(low_done.sem, low_done.at(i, 2))
                        pool.sem_inc(waited.sem, 1)
                        load_lora(ds(i * P + P, P))
                        pool.wait_ge(shifted.sem, shifted.at(i, 3))
                        pool.sem_inc(waited.sem, 1)
                        seed(pool, i, mine, 6)
                        seed(pool, i, mine, 7)
                    pool.wait_ge(exps.sem, exps.at(i, 2))
                    pool.sem_inc(waited.sem, 1)
                    pool.tensor_copy(decays[:, 0:NF], chunked(e_t)[:, :, C - 1]).then_inc(mine.sem, 1)
                    pool.wait_ge(mine.sem, mine.next(i))
                    pool.sem_inc(waited.sem, 1)
                    pool.tensor_copy(decays[:, NF:NF + 1], e_t[:, TP - 1:TP]).then_inc(mine.sem, 1)
                    pool.wait_ge(mine.sem, mine.next(i))
                    pool.sem_inc(waited.sem, 1)
                    pool.tensor_copy(decays[:, NF + 1:NC + NSEQ], seqs(e_t)[:, :, TS - 1]).then_inc(decays_ready.sem, 1)
                    pool.wait_ge(decays_ready.sem, decays_ready.next(i))
                    pool.sem_inc(waited.sem, 1)
                    pool.wait_ge(products.sem, products.at(i, 1))
                    pool.sem_inc(waited.sem, 1)
                    pool.tensor_copy(a8g[:, 0, 0:TAIL], a_r[:, NF, 0:TAIL]).then_inc(mine.sem, 1)
                    pool.wait_ge(mine.sem, mine.next(i))
                    pool.sem_inc(waited.sem, 1)
                    pool.tensor_copy(r_tail[:, 0:TAIL], a_r[:, NF, C:C + TAIL]).then_inc(mine.sem, 1)
                    pool.wait_ge(mine.sem, mine.next(i))
                    pool.sem_inc(waited.sem, 1)
                    pool.tensor_copy(a8[:, C + TAIL:C + TAIL + (C + TS) * NSEQ].rearrange("p (s x) -> p s x", x=C + TS)[:, :, 0:TS],
                                     a_r[:, NF, TAIL:TAIL + NSEQ * TS].rearrange("p (s t) -> p s t", s=NSEQ)).then_inc(a8_ready.sem, 1)
                    pool.wait_ge(a8_ready.sem, a8_ready.next(i))
                    pool.sem_inc(waited.sem, 1)
                    pool.wait_ge(out_read.sem, out_read.at(i, 3))
                    pool.sem_inc(waited.sem, 1)
                    for s in range(NSEQ):
                        pool.dma_start(s_rwkv[0, s, ds(2 * i, 2)].rearrange("h v k -> v h k"),
                                       state_out[0:C, s, :].rearrange("v (h k) -> v h k", h=2)).then_inc(store_s.sem, 16)
                    pool.dma_start(p_rwkv[0, 0, ds(2 * i, 2)].rearrange("h v k -> v h k"),
                                   state_out[0:C, NSEQ, :].rearrange("v (h k) -> v h k", h=2)).then_inc(store_s.sem, 16)
                    pool.wait_ge(store_s.sem, store_s.at(i, 16 * (NSEQ + 1)))
                    pool.sem_inc(waited.sem, 1)
                    pool.wait_ge(merged.sem, merged.at(i, 1))
                    pool.sem_inc(waited.sem, 1)
                    pool.dma_start(m_dram[ds(i, 1)].rearrange("a p t -> (a p) t"), y_t).then_inc(store_m.sem, 16)
                    pool.wait_ge(store_m.sem, store_m.at(i, 16))
                    pool.sem_inc(waited.sem, 1)
                    mine.close()
                with pool.Fori(0, LAST_TURN) as i:
                    turn_of(i)
                turn_of(LAST_TURN, last=True)

            @block.scalar
            def _(act):
                act.sem_inc(pd.half.sem, 3)

                def evacuate(eng, i, mine, t):
                    if t >= 6:
                        eng.wait_ge(pd.evacuated.sem, pd.evacuated.at(i, 12))
                        eng.wait_ge(shifted.sem, shifted.at(i, 3))
                        eng.wait_ge(saved.sem, saved.at(i, 3))
                    eng.wait_ge(seeded.sem, seeded.at(i, t + 1 if t < 6 else t - 2))
                    to_shift_buffer(eng, i, mine, pd, t, z_[t % 2])
                mine, i = s_first, 0
                pd.split_hi(act, i, mine, 0)
                pd.split_hi(act, i, mine, 1)
                evacuate(act, i, mine, 0)
                pd.split_hi(act, i, mine, 2)
                evacuate(act, i, mine, 1)

                def turn_of(i, last=False):
                    recount()
                    mine = s_order
                    all_here(act, i)
                    for n, out in enumerate((lw, a_t)):
                        act.wait_ge(low_done.sem, low_done.at(i, n + 1))
                        act.sem_inc(waited.sem, 1)
                        for half in range(2):
                            signal = low_read if half else mine
                            nc.scalar.activation(out[:, half * HALF:(half + 1) * HALF], bank[2 + 2 * n + half][:, 0:HALF], ACT.Tanh,
                                                 scale=0.5, bias=derived[:, ds(i + 16 * n, 1)]).then_inc(signal.sem, 1)
                            act.wait_ge(signal.sem, signal.next(i))
                            act.sem_inc(waited.sem, 1)
                    pd.split_hi(act, i, mine, 3)
                    act.wait_ge(shifted.sem, shifted.at(i, 1))
                    act.sem_inc(waited.sem, 1)
                    nc.scalar.activation(sq, k_t, ACT.Square, scale=params[:, ds(i + K_K, 1)]).then_inc(k_squared.sem, 1)
                    act.wait_ge(k_squared.sem, k_squared.next(i))
                    act.wait_ge(square_sum.sem, square_sum.at(i, 1))
                    for half in range(2):
                        signal = key_norm if half else mine
                        nc.scalar.activation(sq[:, half * HALF:(half + 1) * HALF], bank[6 + half][:, 0:HALF], ACT.Sqrt).then_inc(signal.sem, 1)
                        act.wait_ge(signal.sem, signal.next(i))
                    act.wait_ge(saved.sem, saved.at(i, 1))
                    evacuate(act, i, mine, 2)
                    act.wait_ge(cum_ready.sem, cum_ready.at(i, 1))
                    nc.scalar.activation(exc, exc, ACT.Exp).then_inc(exps.sem, 1)
                    act.wait_ge(exps.sem, exps.next(i))
                    nc.scalar.activation(e_t, cum, ACT.Exp).then_inc(exps.sem, 1)
                    act.wait_ge(exps.sem, exps.next(i))
                    nc.scalar.activation(cum, cum, ACT.Exp, scale=-1.0).then_inc(exps.sem, 1)
                    act.wait_ge(exps.sem, exps.next(i))
                    pd.split_hi(act, i, mine, 4)

                    def tanh_gate_of(t, out):
                        for half in range(2):
                            act.wait_ge(pd.half.sem, pd.half.at(i, 2 * t + half + 1))
                            nc.scalar.activation(out[:, half * HALF:(half + 1) * HALF], bank[half][:, 0:HALF], ACT.Tanh, scale=0.5).then_inc(tanh_gate.sem, 1)
                            act.wait_ge(tanh_gate.sem, tanh_gate.next(i))
                    tanh_gate_of(3, tg)
                    act.wait_ge(s8_turned.sem, s8_turned.at(i, 1))
                    nc.scalar.copy(s8, bank[6].rearrange("p (s v) -> p s v", s=NSEQ)).then_inc(s8_ready.sem, 1)
                    act.wait_ge(s8_ready.sem, s8_ready.next(i))
                    for c in range(NC):
                        act.wait_ge(turned.sem, turned.at(i, c + 1))
                        nc.scalar.copy(bk_t[:, c, :], bank[4 + c % 2][:, 0:P]).then_inc(mine.sem, 1)
                        act.wait_ge(mine.sem, mine.next(i))
                        nc.scalar.copy(uv[C:P, c, :], bank[4 + c % 2][C:P, P:2 * P]).then_inc(turned_read.sem, 1)
                        act.wait_ge(turned_read.sem, turned_read.next(i))
                    pd.split_hi(act, i, mine, 5)

                    def to_sbuf(out, b, signal):
                        nc.scalar.copy(out[:, 0:NF, :], bank[b].rearrange("p (c t) -> p c t", c=NF)).then_inc(mine.sem, 1)
                        act.wait_ge(mine.sem, mine.next(i))
                        signal = signal or mine
                        nc.scalar.copy(out[:, NF, :], bank[b + 1][:, 0:C]).then_inc(signal.sem, 1)
                        act.wait_ge(signal.sem, signal.next(i))
                    act.wait_ge(from_v_done.sem, from_v_done.at(i, 1))
                    to_sbuf(from_v, 4, from_v_read)
                    for n, out in enumerate((x2, n_d, x2)):
                        act.wait_ge(inv_mm.sem, inv_mm.at(i, n + 1))
                        to_sbuf(out, 6, inv_a)
                    tanh_gate_of(4, tg)
                    if not last:
                        pd.split_hi(act, i, mine, 6)
                    for n in range(2):
                        act.wait_ge(inv_mm.sem, inv_mm.at(i, 5 + 2 * n))
                        to_sbuf(n_d, 4, inv_a)
                    for c in range(NC):
                        if c:
                            act.wait_ge(s_ready.sem, s_ready.at(i, c))
                            nc.scalar.mul(state_decayed, states[:, c - 1, :], decays[:, c:c + 1]).then_inc(decayed.sem, 1)
                            act.wait_ge(decayed.sem, decayed.next(i))
                        else:
                            act.wait_ge(decays_ready.sem, decays_ready.at(i, 1))
                            nc.scalar.mul(state_decayed, eye2, 0.0).then_inc(decayed.sem, 1)
                            act.wait_ge(decayed.sem, decayed.next(i))
                        if c == MERGE_AT:
                            tanh_gate_of(5, tg)
                    act.wait_ge(y_uv.sem, y_uv.at(i, 1))
                    nc.scalar.copy(y_t[:, 0:NF * C], bank[4]).then_inc(mine.sem, 1)
                    act.wait_ge(mine.sem, mine.next(i))
                    nc.scalar.copy(y_t[:, NF * C:T], bank[5][:, 0:LAST]).then_inc(y_copied.sem, 1)
                    act.wait_ge(y_copied.sem, y_copied.next(i))
                    if not last:
                        pd.split_hi(act, i, mine, 7)
                        evacuate(act, i, mine, 6)
                    for n in range(3):
                        act.wait_ge(out_turned.sem, out_turned.at(i, n + 1))
                        w = 4 if n < 2 else 1
                        nc.scalar.copy(state_out[0:C, 4 * n:4 * n + w, :], bank[2 + n % 2][0:C, 0:w * P].rearrange("p (s k) -> p s k", s=w)).then_inc(out_read.sem, 1)
                        act.wait_ge(out_read.sem, out_read.next(i))
                    act.wait_ge(centred.sem, centred.at(i, 1))
                    nc.scalar.activation(e_t, y_t, ACT.Square).then_inc(squared.sem, 1)
                    act.wait_ge(squared.sem, squared.next(i))
                    act.wait_ge(var_done.sem, var_done.at(i, 1))
                    for half in range(2):
                        signal = root if half else mine
                        nc.scalar.activation(e_t[:, half * HALF:(half + 1) * HALF], bank[6 + half][:, 0:HALF], ACT.Sqrt,
                                             scale=1.0 / HEAD, bias=tiny[:, 1:2]).then_inc(signal.sem, 1)
                        act.wait_ge(signal.sem, signal.next(i))
                    if not last:
                        pd.split_hi(act, i, mine, 8)
                        evacuate(act, i, mine, 7)
                        mine.close()
                with act.Fori(0, LAST_TURN) as i:
                    turn_of(i)
                turn_of(LAST_TURN, last=True)

            @block.vector
            def _(dve):
                mine, i = v_order, 0
                for t in range(3):
                    pd.split_lo(dve, i, mine, t)

                def turn_of(i, last=False):
                    recount()
                    mine = v_order
                    tt, stt, ts = dve.tensor_tensor, dve.scalar_tensor_tensor, dve.tensor_scalar
                    col = lambda at: params[:, ds(i + at, 1)]
                    all_here(dve, i)
                    dve.wait_ge(pd.evacuated.sem, pd.evacuated.at(i, 2))
                    dve.wait_ge(seeded.sem, seeded.at(i, 1))
                    token_shift(dve, i, mine, z_[0], k_t, col(MU_K), done=shifted, scratch=exc)
                    dve.wait_ge(low_read.sem, low_read.at(i, 1))
                    ts(lw, lw, 1.0, DECAY, ADD, MUL).then_inc(mine.sem, 1)
                    dve.wait_ge(mine.sem, mine.next(i))
                    dve.tensor_tensor_scan(cum, chunk_start[:, :], lw, 0.0, MUL, ADD).then_inc(mine.sem, 1)
                    dve.wait_ge(mine.sem, mine.next(i))
                    tt(exc, cum, lw, SUB).then_inc(cum_ready.sem, 1)
                    dve.wait_ge(cum_ready.sem, cum_ready.next(i))
                    dve.wait_ge(low_read.sem, low_read.at(i, 2))
                    ts(a_t, a_t, 1.0, 0.5, ADD, MUL).then_inc(mine.sem, 1)
                    dve.wait_ge(mine.sem, mine.next(i))
                    pd.split_lo(dve, i, mine, 3)
                    dve.wait_ge(pd.evacuated.sem, pd.evacuated.at(i, 4))
                    dve.wait_ge(seeded.sem, seeded.at(i, 2))
                    token_shift(dve, i, mine, z_[1], r_t, col(MU_R), done=shifted, scratch=lw)
                    dve.wait_ge(key_norm.sem, key_norm.at(i, 1))
                    ts(sq, sq, 1e-12, None, MAX).then_inc(mine.sem, 1)
                    dve.wait_ge(mine.sem, mine.next(i))
                    dve.reciprocal(sq, sq).then_inc(mine.sem, 1)
                    dve.wait_ge(mine.sem, mine.next(i))
                    stt(out=kk_t, in0=k_t, scalar=col(K_K), in1=sq, op0=MUL, op1=MUL).then_inc(mine.sem, 1)
                    dve.wait_ge(mine.sem, mine.next(i))
                    ts(sq, a_t, col(K_A), derived[:, ds(i + 32, 1)], MUL, ADD).then_inc(mine.sem, 1)
                    dve.wait_ge(mine.sem, mine.next(i))
                    tt(k_t, k_t, sq, MUL).then_inc(mine.sem, 1)
                    dve.wait_ge(mine.sem, mine.next(i))
                    stt(out=sq, in0=r_t, scalar=col(R_K), in1=k_t, op0=MUL, op1=MUL).then_inc(rk_ready.sem, 1)
                    dve.wait_ge(rk_ready.sem, rk_ready.next(i))
                    dve.wait_ge(pd.evacuated.sem, pd.evacuated.at(i, 6))
                    v_t = v_pad[:, C:C + T]
                    token_shift(dve, i, mine, z_[0], v_t, col(MU_V), done=shifted, scratch=lw)
                    dve.wait_ge(exps.sem, exps.at(i, 3))
                    tt(a_t, a_t, kk_t, MUL).then_inc(mine.sem, 1)
                    dve.wait_ge(mine.sem, mine.next(i))

                    for part, (x, e, out, sign) in enumerate(((kk_t, exc, a_r, -1.0), (r_t, e_t, a_r, 1.0), (a_t, cum, b_k, 1.0), (k_t, cum, b_k, 1.0))):
                        o = (part % 2) * C
                        stt(out=out[:, 0:NF, o:o + C], in0=chunked(x), scalar=sign, in1=chunked(e), op0=MUL, op1=MUL).then_inc(mine.sem, 1)
                        dve.wait_ge(mine.sem, mine.next(i))
                        signal = products if part == 3 else mine
                        stt(out=out[:, NF, o:o + LAST], in0=x[:, NF * C:T], scalar=sign, in1=e[:, NF * C:T], op0=MUL, op1=MUL).then_inc(signal.sem, 1)
                        dve.wait_ge(signal.sem, signal.next(i))
                    dve.wait_ge(rk_sum.sem, rk_sum.at(i, 1))
                    for half in range(2):
                        cols = slice(half * HALF, (half + 1) * HALF)
                        signal = bonus_done if half else mine
                        tt(bonus[:, cols], v_t[:, cols], bank[2 + half][:, 0:HALF], MUL).then_inc(signal.sem, 1)
                        dve.wait_ge(signal.sem, signal.next(i))
                    pd.split_lo(dve, i, mine, 4)
                    for half in range(2):
                        dve.wait_ge(tanh_gate.sem, tanh_gate.at(i, half + 1))
                        pd.evacuated.count = 6 + half
                        cols = slice(half * HALF, (half + 1) * HALF)
                        stt(out=gate[:, cols], in0=tg[:, cols], scalar=1.0, in1=bank[half][:, 0:HALF], op0=ADD, op1=MUL).then_inc(pd.evacuated.sem, 1)
                        dve.wait_ge(pd.evacuated.sem, pd.evacuated.next(i))
                    for c in range(NC):
                        dve.wait_ge(gram_done.sem, gram_done.at(i, c + 1))
                        pair = 2 + 4 * (c % 2)
                        tt(gram[:, c, :, :], psum[:, pair:pair + 2, 0:P], bc(causal[:, c // NF, :], 2), MUL).then_inc(gram_read.sem, 1)
                        dve.wait_ge(gram_read.sem, gram_read.next(i))
                    dve.wait_ge(decays_ready.sem, decays_ready.at(i, 1))
                    dve.wait_ge(t_done.sem, t_done.at(i, 1))
                    tt(t_full[:, 0:NF, :], bank[6].rearrange("p (c t) -> p c t", c=NF), bc(lower[:, 0, :], NF), MUL).then_inc(mine.sem, 1)
                    dve.wait_ge(mine.sem, mine.next(i))
                    tt(t_full[:, NF, :], bank[7][:, 0:C], lower[:, 1, :], MUL).then_inc(mine.sem, 1)
                    dve.wait_ge(mine.sem, mine.next(i))
                    tt(t_d, t_full, bc(block16, NC), MUL).then_inc(mine.sem, 1)
                    dve.wait_ge(mine.sem, mine.next(i))
                    for h in range(2):
                        tt(n_d[64 * h:64 * h + 64], gram[0:64, :, h, 0:C], bc(block16[0:64], NC), MUL).then_inc(mine.sem, 1)
                        dve.wait_ge(mine.sem, mine.next(i))
                    tt(inv, n_d, bc(eye2, NC), ADD).then_inc(inv_ready.sem, 1)
                    dve.wait_ge(inv_ready.sem, inv_ready.next(i))
                    pd.split_lo(dve, i, mine, 5)

                    def both(op, signal=None):
                        op(slice(0, NF), lambda b: bank[b].rearrange("p (c t) -> p c t", c=NF)).then_inc(mine.sem, 1)
                        dve.wait_ge(mine.sem, mine.next(i))
                        signal = signal or mine
                        op(NF, lambda b: bank[b + 1][:, 0:C]).then_inc(signal.sem, 1)
                        dve.wait_ge(signal.sem, signal.next(i))
                    for n in range(4):
                        dve.wait_ge(inv_mm.sem, inv_mm.at(i, n + 1))
                        if n < 2:
                            both(lambda c, b: dve.tensor_copy((t2, t_d)[n][:, c, :], b(4)), inv_b)
                        if n > 0:
                            both(lambda c, b: tt(inv[:, c, :], inv[:, c, :], b(2), ADD), inv_b)
                    for half in range(2):
                        dve.wait_ge(tanh_gate.sem, tanh_gate.at(i, half + 3))
                        pd.evacuated.count = 8 + half
                        cols = slice(half * HALF, (half + 1) * HALF)
                        stt(out=gate[:, cols], in0=tg[:, cols], scalar=1.0, in1=gate[:, cols], op0=ADD, op1=MUL).then_inc(pd.evacuated.sem, 1)
                        dve.wait_ge(pd.evacuated.sem, pd.evacuated.next(i))
                    if not last:
                        pd.split_lo(dve, i, mine, 6)
                    for n in range(2):
                        stt(out=t2, in0=inv, scalar=-1.0, in1=bc(eye2, NC), op0=MUL, op1=ADD).then_inc(inv_b.sem, 1)
                        dve.wait_ge(inv_b.sem, inv_b.next(i))
                        dve.wait_ge(inv_mm.sem, inv_mm.at(i, 5 + 2 * n))
                        both(lambda c, b: tt(t2[:, c, :], t2[:, c, :], b(6), ADD), inv_b)
                        dve.wait_ge(inv_mm.sem, inv_mm.at(i, 6 + 2 * n))
                        both(lambda c, b: tt(inv[:, c, :], inv[:, c, :], b(2), ADD), inv_b)
                    for c in range(NC):
                        if c:
                            dve.wait_ge(rhs_done.sem, rhs_done.at(i, c))
                            tt(rhs, bank[7][:, 0:C], from_v[:, c, :], ADD).then_inc(rhs_ready.sem, 1)
                            dve.wait_ge(rhs_ready.sem, rhs_ready.next(i))
                        dve.wait_ge(u_done.sem, u_done.at(i, c + 1))
                        dve.tensor_copy(uv[0:C, c, :].rearrange("p (h k) -> p h k", h=2), psum[0:C, 2:4, 0:C]).then_inc(u_ready.sem, 1)
                        dve.wait_ge(u_ready.sem, u_ready.next(i))
                        if c == NF:
                            for h in range(2):
                                tt(uv8[h], bc(uv[:, NF, 64 * h:64 * h + 64], NC), member.unsqueeze(2).to_broadcast([P, NC, C]), MUL).then_inc(uv8_ready.sem, 1)
                                dve.wait_ge(uv8_ready.sem, uv8_ready.next(i))
                        dve.wait_ge(s_done.sem, s_done.at(i, c + 1))
                        dve.wait_ge(decayed.sem, decayed.at(i, c + 1))
                        stt(out=states[:, c, :], in0=bank[6][:, 0:C], scalar=decays[:, c:c + 1], in1=state_decayed, op0=MUL, op1=ADD).then_inc(s_ready.sem, 1)
                        dve.wait_ge(s_ready.sem, s_ready.next(i))
                        if c == MERGE_AT:
                            dve.wait_ge(load_ob.sem, load_ob.at(i, 16))
                            for half in range(2):
                                dve.wait_ge(tanh_gate.sem, tanh_gate.at(i, half + 5))
                                pd.evacuated.count = 10 + half
                                cols = slice(half * HALF, (half + 1) * HALF)
                                stt(out=ob[:, cols], in0=tg[:, cols], scalar=1.0, in1=ob[:, cols], op0=ADD, op1=MUL).then_inc(pd.evacuated.sem, 1)
                                dve.wait_ge(pd.evacuated.sem, pd.evacuated.next(i))
                    dve.wait_ge(s8_done.sem, s8_done.at(i, 1))
                    tt(s8_new, s8, bank[7].rearrange("p (s v) -> p s v", s=NSEQ), ADD).then_inc(mine.sem, 1)
                    dve.wait_ge(mine.sem, mine.next(i))
                    tt(s8_new, s8_new, decays[:, NC:NC + NSEQ].unsqueeze(2).to_broadcast([P, NSEQ, C]), MUL).then_inc(s8_next.sem, 1)
                    dve.wait_ge(s8_next.sem, s8_next.next(i))
                    dve.wait_ge(y_copied.sem, y_copied.at(i, 1))
                    dve.wait_ge(y_state.sem, y_state.at(i, 1))
                    tt(y_t[:, C:NF * C], y_t[:, C:NF * C], bank[2][:, 0:(NF - 1) * C], ADD).then_inc(mine.sem, 1)
                    dve.wait_ge(mine.sem, mine.next(i))
                    tt(y_t[:, NF * C:T], y_t[:, NF * C:T], bank[3][:, 0:LAST], ADD).then_inc(y_ready.sem, 1)
                    dve.wait_ge(y_ready.sem, y_ready.next(i))
                    if not last:
                        pd.split_lo(dve, i, mine, 7)
                    dve.wait_ge(mean_done.sem, mean_done.at(i, 1))
                    for half in range(2):
                        cols = slice(half * HALF, (half + 1) * HALF)
                        signal = centred if half else mine
                        stt(out=y_t[:, cols], in0=bank[4 + half][:, 0:HALF], scalar=-1.0 / HEAD, in1=y_t[:, cols], op0=MUL, op1=ADD).then_inc(signal.sem, 1)
                        dve.wait_ge(signal.sem, signal.next(i))
                    dve.wait_ge(root.sem, root.at(i, 1))
                    dve.reciprocal(e_t, e_t).then_inc(mine.sem, 1)
                    dve.wait_ge(mine.sem, mine.next(i))
                    tt(y_t, y_t, e_t, MUL).then_inc(mine.sem, 1)
                    dve.wait_ge(mine.sem, mine.next(i))
                    ts(y_t, y_t, col(LN_W), col(LN_B), MUL, ADD).then_inc(mine.sem, 1)
                    dve.wait_ge(mine.sem, mine.next(i))
                    tt(y_t, y_t, bonus, ADD).then_inc(mine.sem, 1)
                    dve.wait_ge(mine.sem, mine.next(i))
                    tt(y_t, y_t, gate, MUL).then_inc(mine.sem, 1)
                    dve.wait_ge(mine.sem, mine.next(i))
                    stt(out=y_t, in0=y_t, scalar=0.25, in1=ob, op0=MUL, op1=ADD).then_inc(merged.sem, 1)
                    dve.wait_ge(merged.sem, merged.next(i))
                    if not last:
                        pd.split_lo(dve, i, mine, 8)
                        mine.close()
                with dve.Fori(0, LAST_TURN) as i:
                    turn_of(i)
                turn_of(LAST_TURN, last=True)

            @block.tensor
            def _(pe):
                pe.wait_ge(masks.sem, masks.count)
                pe.sem_inc(pd.evacuated.sem, 2)
                pd.whole(pe, 0, 0)
                pd.whole(pe, 0, 1)

                def turn_of(i, last=False):
                    all_here(pe, i)
                    mm, tr = pe.matmul, pe.transpose
                    head = [slice(0, 64), slice(64, P)]
                    pe.wait_ge(load_low.sem, load_low.at(i, 32))
                    pe.sem_inc(waited.sem, 1)
                    for n in range(2):
                        for half in range(2):
                            m = mm(bank[2 + 2 * n + half][:, 0:HALF], lora_w[n][0:LORA, :], lora[n][:, half * HALF:(half + 1) * HALF],
                                   start=True, stop=True)
                        m.then_inc(low_done.sem, 1)

                    def head_sums(x, b, signal):
                        for half in range(2):
                            m = mm(bank[b + half][:, 0:HALF], head_ones[:, :], x[:, half * HALF:(half + 1) * HALF], start=True, stop=True)
                        m.then_inc(signal.sem, 1)
                    fill = pd.steps(pe, i, 2)
                    for _ in range(12):
                        next(fill)
                    pe.wait_ge(k_squared.sem, k_squared.at(i, 1))
                    pe.sem_inc(waited.sem, 1)
                    head_sums(sq, 6, square_sum)
                    for _ in fill:
                        pass
                    fill = pd.steps(pe, i, 3)
                    for _ in range(12):
                        next(fill)
                    pe.wait_ge(rk_ready.sem, rk_ready.at(i, 1))
                    pe.sem_inc(waited.sem, 1)
                    head_sums(sq, 2, rk_sum)
                    for _ in fill:
                        pass
                    pe.wait_ge(load_s8.sem, load_s8.at(i, 16 * NSEQ))
                    pe.sem_inc(waited.sem, 1)
                    for s in range(NSEQ):
                        m = tr(bank[6][:, s * C:(s + 1) * C], state8_in[0:C, s, :], ident[0:C, 0:C])
                    m.then_inc(s8_turned.sem, 1)
                    fill = chain(*(pd.steps(pe, i, t) for t in ((4, 5) if last else (4, 5, 6, 7))))

                    def run(n):
                        for _ in range(n):
                            next(fill, None)
                    pe.wait_ge(products.sem, products.at(i, 1))
                    pe.sem_inc(waited.sem, 1)
                    pe.wait_ge(bonus_done.sem, bonus_done.at(i, 1))
                    pe.sem_inc(waited.sem, 1)
                    pe.wait_ge(s8_ready.sem, s8_ready.at(i, 1))
                    pe.sem_inc(waited.sem, 1)
                    for c in range(NC):
                        if c >= 2:
                            pe.wait_ge(gram_read.sem, gram_read.at(i, c - 1))
                            pe.sem_inc(waited.sem, 1)
                            pe.wait_ge(turned_read.sem, turned_read.at(i, c - 1))
                            pe.sem_inc(waited.sem, 1)
                        for h in range(2):
                            m = mm(bank[2 + 4 * (c % 2) + h][:, 0:P], b_k[head[h], c, :], a_r[head[h], c, :], start=True, stop=True)
                        m.then_inc(gram_done.sem, 1)
                        tr(bank[4 + c % 2][:, 0:P], b_k[:, c, :], ident[:, :])
                        tr(bank[4 + c % 2][:, P:2 * P], v_pad[:, c * C:(c + 2) * C], ident[:, :]).then_inc(turned.sem, 1)
                        run(1)

                    def each(b, left, right, signal=None):
                        for c in range(NC):
                            for h in range(2):
                                out = bank[b + c // NF][head[h], c % NF * C:(c % NF + 1) * C]
                                m = mm(out, left(c)[head[h]], right(c)[head[h]], start=True, stop=True)
                        if signal:
                            m.then_inc(signal.sem, 1)
                    of = lambda x: (lambda c: x[:, c, :])
                    pe.wait_ge(gram_read.sem, gram_read.at(i, NC))
                    pe.sem_inc(waited.sem, 1)
                    pe.wait_ge(turned_read.sem, turned_read.at(i, NC))
                    pe.sem_inc(waited.sem, 1)
                    each(6, lambda c: a_r[:, c, 0:C], lambda c: b_k[:, c, 0:C], t_done)
                    for c in range(NC):
                        for h in range(2):
                            m = mm(bank[4 + c // NF][head[h], c % NF * C:(c % NF + 1) * C], gram[C:P, c, h, 0:C],
                                   uv[C:P, c, 64 * h:64 * h + 64], start=True, stop=True)
                    m.then_inc(from_v_done.sem, 1)
                    run(7)
                    pe.wait_ge(inv_ready.sem, inv_ready.at(i, 1))
                    pe.sem_inc(waited.sem, 1)
                    pe.wait_ge(from_v_read.sem, from_v_read.at(i, 1))
                    pe.sem_inc(waited.sem, 1)
                    each(6, of(t_d), of(n_d))
                    run(1)
                    each(4, of(n_d), of(t_d), inv_mm)
                    run(1)
                    run(2)
                    pe.wait_ge(inv_a.sem, inv_a.at(i, 1))
                    pe.sem_inc(waited.sem, 1)
                    pe.wait_ge(inv_b.sem, inv_b.at(i, 1))
                    pe.sem_inc(waited.sem, 1)
                    each(6, of(t2), of(x2))
                    run(1)
                    each(4, of(x2), of(t2))
                    run(1)
                    each(2, of(t2), of(inv), inv_mm)
                    run(1)
                    run(2)
                    pe.wait_ge(inv_a.sem, inv_a.at(i, 2))
                    pe.sem_inc(waited.sem, 1)
                    pe.wait_ge(inv_b.sem, inv_b.at(i, 3))
                    pe.sem_inc(waited.sem, 1)
                    each(6, of(n_d), of(t_d))
                    run(1)
                    each(2, of(t_d), of(inv), inv_mm)
                    run(1)
                    run(2)
                    pe.wait_ge(inv_a.sem, inv_a.at(i, 3))
                    pe.sem_inc(waited.sem, 1)
                    pe.wait_ge(inv_b.sem, inv_b.at(i, 4))
                    pe.sem_inc(waited.sem, 1)
                    each(2, of(x2), of(inv), inv_mm)
                    run(1)
                    for n in range(2):
                        run(2 + n)
                        pe.wait_ge(inv_b.sem, inv_b.at(i, 6 + 3 * n - 1))
                        pe.sem_inc(waited.sem, 1)
                        each(6, of(t_full), of(inv))
                        run(1)
                        each(4, of(inv), lambda c: eye2, inv_mm)
                        run(1)
                        run(3)
                        pe.wait_ge(inv_b.sem, inv_b.at(i, 7 + 3 * n))
                        pe.sem_inc(waited.sem, 1)
                        pe.wait_ge(inv_a.sem, inv_a.at(i, 4 + n))
                        pe.sem_inc(waited.sem, 1)
                        each(2, of(n_d), of(t2), inv_mm)
                        run(1)
                    run(3)
                    pe.wait_ge(inv_b.sem, inv_b.at(i, 11))
                    pe.sem_inc(waited.sem, 1)
                    for c in range(NC):
                        if c:
                            pe.wait_ge(s_ready.sem, s_ready.at(i, c))
                            pe.sem_inc(waited.sem, 1)
                        if c and c < NF:
                            for h in range(2):
                                m = mm(bank[7][head[h], 0:C], a_r[head[h], c, 0:C], states[head[h], c - 1, :], start=True, stop=True)
                        elif c == NF:
                            pe.wait_ge(a8_ready.sem, a8_ready.at(i, 1))
                            pe.sem_inc(waited.sem, 1)
                            for h in range(2):
                                for g in range(NC):
                                    s = states[head[h], c - 1, :] if g == 0 else s8[head[h], g - 1, :]
                                    m = mm(bank[7][head[h], 0:C], a8g[head[h], g, :], s, start=(g == 0), stop=(g == NC - 1), skip_group_check=True)
                        if c:
                            m.then_inc(rhs_done.sem, 1)
                        run(1)
                        if c:
                            pe.wait_ge(rhs_ready.sem, rhs_ready.at(i, c))
                            pe.sem_inc(waited.sem, 1)
                        for h in range(2):
                            right = rhs[head[h], :] if c else from_v[head[h], 0, :]
                            m = mm(bank[2 + h][0:C, 0:C], inv[head[h], c, :], right, start=True, stop=True)
                        m.then_inc(u_done.sem, 1)
                        run(1)
                        pe.wait_ge(u_ready.sem, u_ready.at(i, c + 1))
                        pe.sem_inc(waited.sem, 1)
                        if c < NF:
                            for h in range(2):
                                m = mm(bank[6][head[h], 0:C], bk_t[:, c, 64 * h:64 * h + 64], uv[:, c, 64 * h:64 * h + 64], start=True, stop=True)
                        else:
                            for h in range(2):
                                pe.wait_ge(uv8_ready.sem, uv8_ready.at(i, h + 1))
                                pe.sem_inc(waited.sem, 1)
                                m = mm(bank[6][head[h], 0:C], bk_t[:, c, 64 * h:64 * h + 64], uv8[h][:, 0, :], start=True, stop=True)
                        m.then_inc(s_done.sem, 1)
                        w = C if c < NF else LAST
                        for h in range(2):
                            m = mm(bank[4 + c // NF][head[h], c % NF * C:c % NF * C + w], uv[:, c, 64 * h:64 * h + 64],
                                   gram[:, c, h, C:C + w], start=True, stop=True)
                        if c == NF:
                            m.then_inc(y_uv.sem, 1)
                        run(2)
                    for h in range(2):
                        m = mm(bank[7][head[h], :], bk_t[:, NF, 64 * h:64 * h + 64], uv8[h][:, 1:NC, :], start=True, stop=True)
                    m.then_inc(s8_done.sem, 1)
                    for h in range(2):
                        for c in range(1, NF):
                            mm(bank[2][head[h], (c - 1) * C:c * C], states[head[h], c - 1, :], a_r[head[h], c, C:P], start=True, stop=True)
                        mm(bank[3][head[h], 0:LAST], states[head[h], NF - 1, :], r_tail[head[h], :], start=True, stop=False,
                           skip_group_check=True)
                        for s in range(NSEQ):
                            at = TAIL + s * TS
                            m = mm(bank[3][head[h], at:at + TS], s8[head[h], s, :], a_r[head[h], NF, C + at:C + at + TS], start=False,
                                   stop=(s == NSEQ - 1), skip_group_check=True)
                    m.then_inc(y_state.sem, 1)
                    run(10)
                    pe.wait_ge(s_ready.sem, s_ready.at(i, NC))
                    pe.sem_inc(waited.sem, 1)
                    pe.wait_ge(s8_next.sem, s8_next.at(i, 1))
                    pe.sem_inc(waited.sem, 1)
                    pe.wait_ge(y_ready.sem, y_ready.at(i, 1))
                    pe.sem_inc(waited.sem, 1)
                    head_sums(y_t, 4, mean_done)
                    run(20)
                    for n in range(3):
                        if n == 2:
                            pe.wait_ge(out_read.sem, out_read.at(i, 1))
                            pe.sem_inc(waited.sem, 1)
                        for s in range(4 if n < 2 else 1):
                            src = s8_new[:, 4 * n + s, :] if n < 2 else states[:, NF, :]
                            m = tr(bank[2 + n % 2][0:C, s * P:(s + 1) * P], src, ident[:, :])
                        m.then_inc(out_turned.sem, 1)
                    pe.wait_ge(squared.sem, squared.at(i, 1))
                    pe.sem_inc(waited.sem, 1)
                    head_sums(e_t, 6, var_done)
                    for _ in fill:
                        pass
                with pe.Fori(0, LAST_TURN) as i:
                    turn_of(i)
                turn_of(LAST_TURN, last=True)


        ar = Arena()
        o_rows = ar(5, D)
        ar.at = 0
        m_in = ar(NPAIR, T)
        ar.at = 5 * D
        x_rows = [ar(D) for _ in range(3)]
        norm_row = ar(D)
        o_t = [ar(TOK) for _ in range(2)]
        shift_rows = x_rows[2][0:48, 0:9 * P]
        lora_rows = ar(LORA)
        stats = ar(16)
        pe_ = Projection("e", 2)

        def again(*signals):
            for s in signals:
                s.count -= s.per
        v_order, s_order, a_order = sig("e_vector"), sig("e_scalar"), sig("e_scalar_loop")
        d_order = sig("e_vector_loop", DED)
        load_m, m_hi, m_lo = [sig(f"e_load_m{n}") for n in range(4)], sig("e_m_hi"), sig("e_m_lo")
        shift_turned, shift_ready, store_shift = sig("e_shift_turned"), sig("e_shift_ready"), sig("e_store_shift")
        o_turned, o_taken = sig("e_o_turned", 4), sig("e_o_taken", 4)
        o_turned.bias, o_taken.bias = 3, 2
        load_norm, load_x = sig("e_load_norm"), [sig(f"e_load_x{n}") for n in range(5)]
        summed, rooted, y_rows, store_y = sig("e_square_sum"), sig("e_root"), sig("e_y"), sig("e_store_y")
        TURNS = NPAIR // 2
        token_rows = [(t, P if t < 4 else NSEQ * TS) for t in range(5)]
        with nc.Block() as block:
            @block.sync
            def _(sp):
                for n in range(4):
                    sp.dma_start(m_in[:, 4 * n:4 * n + 4, :], m_dram[4 * n:4 * n + 4].rearrange("j p t -> p j t")).then_inc(load_m[n].sem, 16)
                sp.sem_inc(pe_.lo.sem, 2)
                with sp.Fori(0, TURNS) as i:
                    for t in range(2):
                        pe_.load(sp, i, t, lambda h: w_out[0, h * D // 2:(h + 1) * D // 2, ds(i * 2 * P + t * P, P)])
                for t, n in token_rows:
                    if t < 4:
                        sp.wait_ge(y_rows.sem, t + 1)
                        sp.dma_start(y_prompt[0, t * P:(t + 1) * P, :], o_rows[:, t, :]).then_inc(store_y.sem, 16)
                    else:
                        sp.wait_ge(y_rows.sem, t + 1)
                        sp.dma_start(y_sample.rearrange("s t d -> (s t) d"), o_rows[0:n, t, :]).then_inc(store_y.sem, 16)
                sp.wait_ge(store_y.sem, 16 * 5)

            @block.gpsimd
            def _(pool):
                pool.dma_start(norm_row, norm_post[0:1, :].to_broadcast([P, D])).then_inc(load_norm.sem, 16)
                pool.wait_ge(shift_ready.sem, 4)
                rows = shift_rows.rearrange("j (s c) -> j s c", s=9)
                pool.dma_start(p_shift[0, 0, 0:3 * D].rearrange("(j c) -> j c", c=P), rows[:, 0, :]).then_inc(store_shift.sem, 16)
                for s in range(NSEQ):
                    pool.dma_start(s_shift[0, s, 0:3 * D].rearrange("(j c) -> j c", c=P), rows[:, 1 + s, :]).then_inc(store_shift.sem, 16)
                for j in range(2):
                    cols = slice(3 * D + j * LORA, 3 * D + (j + 1) * LORA)
                    pool.dma_start(p_shift[0, :, cols], lora_rows[9 * j:9 * j + 1]).then_inc(store_shift.sem, 16)
                    pool.dma_start(s_shift[0, :, cols], lora_rows[9 * j + 1:9 * j + 9]).then_inc(store_shift.sem, 16)
                for t, n in token_rows:
                    if t == 2:
                        pool.wait_ge(store_shift.sem, 16 * (NSEQ + 5))
                    if t >= 3:
                        pool.wait_ge(y_rows.sem, t - 2)
                    src = x_prompt[0, t * P:(t + 1) * P, :] if t < 4 else x_sample.rearrange("s t d -> (s t) d")
                    pool.dma_start(x_rows[t % 3][0:n, :], src).then_inc(load_x[t].sem, 16)

            @block.scalar
            def _(act):
                mine, i = s_order, 0
                for n in range(4):
                    act.wait_ge(shift_turned.sem, shift_turned.at(i, n + 1))
                    if n < 3:
                        w = 4 if n < 2 else 1
                        nc.scalar.copy(shift_rows[:, 4 * n * P:(4 * n + w) * P], bank[4 + n][0:48, 0:w * P]).then_inc(shift_ready.sem, 1)
                        act.wait_ge(shift_ready.sem, shift_ready.next(i))
                    else:
                        nc.scalar.copy(lora_rows[0:18, 0:LORA], bank[7][0:18, 0:LORA]).then_inc(shift_ready.sem, 1)
                        act.wait_ge(shift_ready.sem, shift_ready.next(i))
                for j in range(NPAIR):
                    act.wait_ge(load_m[j // 4].sem, load_m[j // 4].at(i, 16))
                    nc.scalar.copy(act_hi[:, j, :], m_in[:, j, :]).then_inc(m_hi.sem, 1)
                    act.wait_ge(m_hi.sem, m_hi.next(i))
                act.sem_inc(pe_.half.sem, 3)
                pe_.split_hi(act, 0, a_order, 0)

                def turn(i, last=False):
                    mine = a_order
                    for t in range(2):
                        if not (last and t):
                            pe_.split_hi(act, i, mine, t + 1)
                        for half in range(2):
                            act.wait_ge(pe_.half.sem, pe_.half.at(i, 2 * t + half + 1))
                            if half == 0:
                                act.wait_ge(o_turned.sem, o_turned.at(i, 2 * t - 2))
                            nc.scalar.copy(o_t[t][:, half * TOK // 2:(half + 1) * TOK // 2], bank[half][:, 0:TOK // 2]).then_inc(pe_.evacuated.sem, 1)
                            act.wait_ge(pe_.evacuated.sem, pe_.evacuated.next(i))
                with act.Fori(0, TURNS - 1) as i:
                    turn(i)
                again(pe_.hi, pe_.evacuated)
                turn(TURNS - 1, last=True)
                mine, i = s_order, 0
                act.wait_ge(o_taken.sem, o_taken.at(i, 4 * TURNS))
                for t, n in token_rows:
                    nc.scalar.activation(psum[0:n, 0:4, :], o_rows[0:n, t, :].rearrange("p (a b) -> p a b", a=4), ACT.Square,
                                         accum_out=stats[0:n, t:t + 1]).then_inc(summed.sem, 1)
                    act.wait_ge(summed.sem, summed.next(i))
                    nc.scalar.activation(stats[0:n, 5 + t:6 + t], stats[0:n, t:t + 1], ACT.Sqrt, scale=1.0 / D, bias=tiny[0:n, 0:1]).then_inc(rooted.sem, 1)
                    act.wait_ge(rooted.sem, rooted.next(i))

            @block.vector
            def _(dve):
                mine, i = v_order, 0
                for j in range(NPAIR):
                    dve.wait_ge(m_hi.sem, m_hi.at(i, j + 1))
                    dve.tensor_tensor(act_lo[:, j, :], m_in[:, j, :], act_hi[:, j, :].bitcast(F32), SUB).then_inc(m_lo.sem, 1)
                    dve.wait_ge(m_lo.sem, m_lo.next(i))
                pe_.split_lo(dve, 0, d_order, 0)

                def turn(i, last=False):
                    mine = d_order
                    for t in range(2):
                        if not (last and t):
                            pe_.split_lo(dve, i, mine, t + 1)
                        for part, (b, tt_, n) in enumerate(((4, slice(0, 2), P), (6, slice(2, 4), P))):
                            dve.wait_ge(o_turned.sem, o_turned.at(i, 2 * t + part + 1))
                            dve.sem_inc(waited.sem, 1)
                            col = ds(i * 2 * P + t * P, P)
                            signal = mine if part else o_taken
                            dve.tensor_copy(o_rows[:, tt_, col], bank[b][:, 0:2 * P].rearrange("p (a c) -> p a c", a=2)).then_inc(signal.sem, 1)
                            dve.wait_ge(signal.sem, signal.next(i))
                            if part:
                                dve.sem_inc(waited.sem, 1)
                                dve.tensor_copy(o_rows[0:32, 4, col], bank[b][0:32, 2 * P:3 * P]).then_inc(o_taken.sem, 1)
                                dve.wait_ge(o_taken.sem, o_taken.next(i))
                with dve.Fori(0, TURNS - 1) as i:
                    turn(i)
                    d_order.close()
                again(pe_.lo, o_taken, d_order)
                turn(TURNS - 1, last=True)
                mine, i = v_order, 0
                dve.wait_ge(load_norm.sem, load_norm.at(i, 16))
                for t, n in token_rows:
                    dve.wait_ge(rooted.sem, rooted.at(i, t + 1))
                    dve.reciprocal(stats[0:n, 10 + t:11 + t], stats[0:n, 5 + t:6 + t]).then_inc(mine.sem, 1)
                    dve.wait_ge(mine.sem, mine.next(i))
                    o = o_rows[0:n, t, :]
                    dve.scalar_tensor_tensor(out=o, in0=o, scalar=stats[0:n, 10 + t:11 + t], in1=norm_row[0:n, :], op0=MUL, op1=MUL).then_inc(mine.sem, 1)
                    dve.wait_ge(mine.sem, mine.next(i))
                    dve.wait_ge(load_x[t].sem, load_x[t].at(i, 16))
                    dve.tensor_tensor(o, o, x_rows[t % 3][0:n, :], ADD).then_inc(y_rows.sem, 1)
                    dve.wait_ge(y_rows.sem, y_rows.next(i))

            @block.tensor
            def _(pe):
                for n in range(3):
                    for s in range(4 * n, min(4 * n + 4, 9)):
                        m = pe.transpose(bank[4 + n][0:48, (s - 4 * n) * P:(s - 4 * n + 1) * P], shift_out[:, 0:48, s], ident[:, :])
                    m.then_inc(shift_turned.sem, 1)
                pe.transpose(bank[7][0:18, 0:LORA], shift_out[0:LORA, 48:50, :].rearrange("p j s -> p (j s)"), ident[0:LORA, 0:LORA]).then_inc(
                    shift_turned.sem, 1)
                pe.wait_ge(shift_ready.sem, 4)
                pe.sem_inc(pe_.evacuated.sem, 2)
                pe.sem_inc(o_turned.sem, 3)
                pe.sem_inc(o_taken.sem, 2)
                pe.wait_ge(m_lo.sem, NPAIR)
                with pe.Fori(0, TURNS) as i:
                    def turn(t, part):
                        pe.wait_ge(pe_.evacuated.sem, pe_.evacuated.at(i, 2 * t + 1 + part))
                        pe.sem_inc(waited.sem, 1)
                        pe.wait_ge(o_taken.sem, o_taken.at(i, 2 * t + part - 1))
                        pe.sem_inc(waited.sem, 1)
                        for n, tok in enumerate(((0, 1), (2, 3, 4))[part]):
                            w = P if tok < 4 else 32
                            m = pe.transpose(bank[4 + 2 * part][0:w, n * P:(n + 1) * P], o_t[t][:, tok * P:tok * P + w], ident[:, :])
                        m.then_inc(o_turned.sem, 1)
                    for t in range(2):
                        for step, _ in enumerate(pe_.steps(pe, i, t, first=META, tokens=TOK // 2)):
                            if t and step == 8:
                                turn(0, 1)
                            if step == 26:
                                turn(t, 0)
                    turn(1, 1)


def kernel(**inputs):
    import concourse.bacc as bacc
    from concourse.bass_utils import run_bass_kernel_spmd
    data = {name: np.ascontiguousarray(np.asarray(value)) for name, value in inputs.items()}
    shapes = dict(
        y_prompt=(1, SEQ, D), y_sample=(NSEQ, TS, D), p_rwkv=(1, 1, 2 * NPAIR, HEAD, HEAD), p_shift=(1, 1, SHIFT),
        p_gla=(1, 1, BH, BK_, BV), s_rwkv=(1, NSEQ, 2 * NPAIR, HEAD, HEAD), s_shift=(1, NSEQ, SHIFT), s_gla=(1, NSEQ, BH, BK_, BV))
    nc = bacc.Bacc("TRN2", target_bir_lowering=False, num_devices=1)
    aps = {name: nc.dram_tensor(f"in_{name}_dram", value.shape, F32, kind="ExternalInput").ap() for name, value in data.items()}
    aps |= {name: nc.dram_tensor(f"out_{name}_dram", shape, F32, kind="ExternalOutput").ap() for name, shape in shapes.items()}
    build(nc, **aps)
    if not nc.is_finalized():
        nc.finalize()
    result = run_bass_kernel_spmd(nc, [{f"in_{name}_dram": value for name, value in data.items()}], core_ids=[0])
    return tuple(result.results[0][f"out_{name}_dram"] for name in shapes)
```
